# Optimizing a Trainium2 kernel written in Bass

```python
import math
import jax
import jax.numpy as jnp
from jax import lax
import numpy as np
import jax, jax.numpy as jnp

D_MODEL = 1024
BATCH = 1
SEQ = 256
DEPTH = 2

D_MIX = D_MODEL
HG_HEADS = 4
HG_DK = 64
HG_DV = 64
HG_QK = HG_HEADS * HG_DK
HG_W = HG_HEADS * HG_DV
GD_HEADS = 4
GD_DK = 128
GD_DV = 128
GD_QK = GD_HEADS * GD_DK
GD_W = GD_HEADS * GD_DV
RG_W = D_MIX - HG_W - GD_W
RG_BLOCKS = 4
RG_BD = RG_W // RG_BLOCKS
RG_C = 8.0
CONV_W = 4
D_FF = 2816
CHUNK = 64
EPS = 1e-6
SPLIT_SIZES = (HG_QK, HG_QK, HG_W, HG_W, GD_QK, GD_QK, GD_W, GD_W, GD_HEADS, GD_HEADS, RG_W, RG_W)
SPLIT_POINTS = tuple(int(p) for p in np.cumsum(SPLIT_SIZES)[:-1])
N_IN = int(sum(SPLIT_SIZES))


def rmsnorm(x, w):
    xf = x.astype(jnp.float32)
    y = xf * lax.rsqrt(jnp.mean(xf * xf, axis=-1, keepdims=True) + EPS)
    return (y * w.astype(jnp.float32)).astype(x.dtype)

def head_rmsnorm(o, w):
    return o * lax.rsqrt(jnp.mean(o * o, axis=-1, keepdims=True) + EPS) * w.astype(jnp.float32)

def l2norm(t):
    return t * lax.rsqrt(jnp.sum(t * t, axis=-1, keepdims=True) + EPS)

def causal_depthwise_conv(x, w):
    return lax.conv_general_dilated(
        x, w[:, None, :].astype(x.dtype), window_strides=(1,), padding=[(CONV_W - 1, 0)],
        dimension_numbers=('NWC', 'WIO', 'NWC'), feature_group_count=x.shape[-1])

def to_chunks(t):
    b, l, h, d = t.shape
    return t.reshape(b, l // CHUNK, CHUNK, h, d).transpose(1, 0, 3, 2, 4)

def from_chunks(t):
    n, b, h, c, d = t.shape
    return t.transpose(1, 0, 3, 2, 4).reshape(b, n * c, h, d)

def swiglu(h, w_gate, w_up, w_down):
    return (jax.nn.silu(h @ w_gate) * (h @ w_up)) @ w_down

def hgrn2_chunked(q, k, v, logf):
    qc, kc, vc, gc = to_chunks(q), to_chunks(k), to_chunks(v), to_chunks(logf)
    _, b, h, _, dk = qc.shape
    dv = vc.shape[-1]
    causal = jnp.tril(jnp.ones((CHUNK, CHUNK), dtype=bool))[:, :, None]

    def step(state, inp):
        qi, ki, vi, gi = inp
        cum = jnp.cumsum(gi, axis=2)
        diff = cum[:, :, :, None, :] - cum[:, :, None, :, :]
        decay = jnp.exp(jnp.where(causal, diff, -jnp.inf))
        scores = jnp.einsum('bhtd,bhsd,bhtsd->bhts', qi, ki, decay)
        o = (jnp.einsum('bhts,bhsv->bhtv', scores, vi)
             + jnp.einsum('bhtd,bhdv->bhtv', qi * jnp.exp(cum), state))
        last = cum[:, :, -1:, :]
        state = (state * jnp.exp(last[:, :, 0, :, None])
                 + jnp.einsum('bhsd,bhsv->bhdv', ki * jnp.exp(last - cum), vi))
        return state, o

    s0 = jnp.zeros((b, h, dk, dv), jnp.float32)
    _, o = lax.scan(step, s0, (qc, kc, vc, gc))
    return from_chunks(o)

def gated_delta_chunked(q, k, v, g, beta):
    qc, kc, vc = to_chunks(q), to_chunks(k), to_chunks(v)
    gc = to_chunks(g[..., None])[..., 0]
    bc = to_chunks(beta[..., None])[..., 0]
    _, b, h, _, dk = qc.shape
    dv = vc.shape[-1]
    incl = jnp.tril(jnp.ones((CHUNK, CHUNK), dtype=bool))
    strict = jnp.tril(jnp.ones((CHUNK, CHUNK), dtype=bool), k=-1)
    eye = jnp.eye(CHUNK, dtype=jnp.float32)

    def step(state, inp):
        qi, ki, vi, gi, bi = inp
        cum = jnp.cumsum(gi, axis=-1)
        decay = jnp.exp(jnp.where(incl, cum[..., :, None] - cum[..., None, :], -jnp.inf))
        kb = ki * bi[..., None]
        lower = jnp.where(strict, jnp.einsum('bhtd,bhsd->bhts', kb, ki) * decay, 0.0)
        rhs = jnp.concatenate([vi * bi[..., None], kb * jnp.exp(cum)[..., None]], axis=-1)
        sol = lax.linalg.triangular_solve(eye + lower, rhs, left_side=True, lower=True,
                                          unit_diagonal=True)
        u, w = sol[..., :dv], sol[..., dv:]
        v_new = u - jnp.einsum('bhtd,bhdv->bhtv', w, state)
        scores = jnp.einsum('bhtd,bhsd->bhts', qi, ki) * decay
        o = (jnp.einsum('bhtd,bhdv->bhtv', qi * jnp.exp(cum)[..., None], state)
             + jnp.einsum('bhts,bhsv->bhtv', scores, v_new))
        last = cum[..., -1:]
        state = (state * jnp.exp(last)[..., None]
                 + jnp.einsum('bhsd,bhsv->bhdv', ki * jnp.exp(last - cum)[..., None], v_new))
        return state, o

    s0 = jnp.zeros((b, h, dk, dv), jnp.float32)
    _, o = lax.scan(step, s0, (qc, kc, vc, gc, bc))
    return from_chunks(o)

def rg_lru(xc, wr, br, wi, bi, lam):
    b, l, _ = xc.shape
    xb = xc.reshape(b, l, RG_BLOCKS, RG_BD)
    r = jax.nn.sigmoid(jnp.einsum('blni,nio->blno', xb, wr.astype(jnp.float32)).reshape(b, l, RG_W)
                       + br.astype(jnp.float32))
    ig = jax.nn.sigmoid(jnp.einsum('blni,nio->blno', xb, wi.astype(jnp.float32)).reshape(b, l, RG_W)
                        + bi.astype(jnp.float32))
    log_a = -RG_C * r * jax.nn.softplus(-lam.astype(jnp.float32))
    a = jnp.exp(log_a)
    bx = jnp.sqrt(-jnp.expm1(2.0 * log_a)) * (ig * xc)

    def combine(c1, c2):
        a1, b1 = c1
        a2, b2 = c2
        return a1 * a2, a2 * b1 + b2

    _, hs = lax.associative_scan(combine, (a, bx), axis=1)
    return hs

def hybrid_mixer(h, lb, w_in, hg_norm_w, gd_conv_w, gd_a_log, gd_dt_bias, gd_norm_w,
                 rg_conv_w, rg_conv_b, rg_wr, rg_br, rg_wi, rg_bi, rg_lambda, w_out):
    b, l, _ = h.shape
    f32 = jnp.float32
    proj = (h @ w_in).astype(f32)
    (hg_q, hg_f, hg_i, hg_g, gd_q, gd_k, gd_v, gd_z, gd_b, gd_a,
     rg_x, rg_gate) = jnp.split(proj, SPLIT_POINTS, axis=-1)

    lbf = lb.reshape(HG_HEADS, HG_DK)
    q = jax.nn.silu(hg_q).reshape(b, l, HG_HEADS, HG_DK) * (HG_DK ** -0.5)
    f = lbf + (1.0 - lbf) * jax.nn.sigmoid(hg_f.reshape(b, l, HG_HEADS, HG_DK))
    o_hg = hgrn2_chunked(q, 1.0 - f, hg_i.reshape(b, l, HG_HEADS, HG_DV), jnp.log(f))
    o_hg = head_rmsnorm(o_hg, hg_norm_w) * jax.nn.silu(hg_g.reshape(b, l, HG_HEADS, HG_DV))

    qkv = jax.nn.silu(causal_depthwise_conv(jnp.concatenate([gd_q, gd_k, gd_v], axis=-1), gd_conv_w))
    cq, ck, cv = jnp.split(qkv, (GD_QK, 2 * GD_QK), axis=-1)
    cq = l2norm(cq.reshape(b, l, GD_HEADS, GD_DK)) * (GD_DK ** -0.5)
    ck = l2norm(ck.reshape(b, l, GD_HEADS, GD_DK))
    beta = jax.nn.sigmoid(gd_b)
    g = -jnp.exp(gd_a_log.astype(f32)) * jax.nn.softplus(gd_a + gd_dt_bias.astype(f32))
    o_gd = gated_delta_chunked(cq, ck, cv.reshape(b, l, GD_HEADS, GD_DV), g, beta)
    o_gd = head_rmsnorm(o_gd, gd_norm_w) * jax.nn.silu(gd_z.reshape(b, l, GD_HEADS, GD_DV))

    xc = causal_depthwise_conv(rg_x, rg_conv_w) + rg_conv_b.astype(f32)
    o_rg = rg_lru(xc, rg_wr, rg_br, rg_wi, rg_bi, rg_lambda) * jax.nn.gelu(rg_gate, approximate=True)

    y = jnp.concatenate([o_hg.reshape(b, l, HG_W), o_gd.reshape(b, l, GD_W), o_rg], axis=-1)
    return y.astype(h.dtype) @ w_out

def first_inputs(seed: int = 0) -> dict:
    key = jax.random.key(seed)
    ks = jax.random.split(key, 32)
    f32 = jnp.float32

    def nrm(k, shape, scale):
        return jax.random.normal(k, shape, f32) * scale

    def gain(k, shape):
        return 1.0 + 0.02 * jax.random.normal(k, shape, f32)

    dt = jnp.exp(jax.random.uniform(ks[12], (DEPTH, GD_HEADS), f32, math.log(1e-3), math.log(1e-1)))
    a0 = jax.random.uniform(ks[19], (DEPTH, RG_W), f32, 0.9, 0.999) ** (1.0 / RG_C)
    return {
        'x': nrm(ks[0], (BATCH, SEQ, D_MODEL), 1.0),
        'norm_ffn1': gain(ks[1], (DEPTH, D_MODEL)),
        'ffn1_gate': nrm(ks[2], (DEPTH, D_MODEL, D_FF), D_MODEL ** -0.5),
        'ffn1_up': nrm(ks[3], (DEPTH, D_MODEL, D_FF), D_MODEL ** -0.5),
        'ffn1_down': nrm(ks[4], (DEPTH, D_FF, D_MODEL), D_FF ** -0.5),
        'norm_mix': gain(ks[5], (DEPTH, D_MODEL)),
        'w_in': nrm(ks[6], (DEPTH, D_MODEL, N_IN), D_MODEL ** -0.5),
        'hg_lb': nrm(ks[7], (DEPTH, HG_QK), 1.0),
        'hg_norm_w': gain(ks[8], (DEPTH, HG_DV)),
        'gd_conv_w': nrm(ks[9], (DEPTH, CONV_W, 2 * GD_QK + GD_W), CONV_W ** -0.5),
        'gd_a_log': jnp.log(jax.random.uniform(ks[10], (DEPTH, GD_HEADS), f32, 1.0, 16.0)),
        'gd_dt_bias': dt + jnp.log(-jnp.expm1(-dt)),
        'gd_norm_w': gain(ks[11], (DEPTH, GD_DV)),
        'rg_conv_w': nrm(ks[13], (DEPTH, CONV_W, RG_W), CONV_W ** -0.5),
        'rg_conv_b': nrm(ks[14], (DEPTH, RG_W), 0.02),
        'rg_wr': nrm(ks[15], (DEPTH, RG_BLOCKS, RG_BD, RG_BD), RG_BD ** -0.5),
        'rg_br': nrm(ks[16], (DEPTH, RG_W), 0.1),
        'rg_wi': nrm(ks[17], (DEPTH, RG_BLOCKS, RG_BD, RG_BD), RG_BD ** -0.5),
        'rg_bi': nrm(ks[18], (DEPTH, RG_W), 0.1),
        'rg_lambda': jnp.log(a0) - jnp.log1p(-a0),
        'w_out': nrm(ks[20], (DEPTH, D_MIX, D_MODEL), D_MIX ** -0.5),
        'norm_ffn2': gain(ks[21], (DEPTH, D_MODEL)),
        'ffn2_gate': nrm(ks[22], (DEPTH, D_MODEL, D_FF), D_MODEL ** -0.5),
        'ffn2_up': nrm(ks[23], (DEPTH, D_MODEL, D_FF), D_MODEL ** -0.5),
        'ffn2_down': nrm(ks[24], (DEPTH, D_FF, D_MODEL), D_FF ** -0.5),
        'norm_final': gain(ks[25], (D_MODEL,)),
    }

def first_block(x, norm_ffn1, ffn1_gate, ffn1_up, ffn1_down, norm_mix, w_in, hg_lb, hg_norm_w,
              gd_conv_w, gd_a_log, gd_dt_bias, gd_norm_w, rg_conv_w, rg_conv_b, rg_wr, rg_br,
              rg_wi, rg_bi, rg_lambda, w_out, norm_ffn2, ffn2_gate, ffn2_up, ffn2_down, norm_final):
    lb_all = jnp.cumsum(jax.nn.softmax(hg_lb.astype(jnp.float32), axis=0), axis=0)
    lb_all = lb_all - lb_all[0]
    for layer in range(DEPTH):
        x = x + 0.5 * swiglu(rmsnorm(x, norm_ffn1[layer]), ffn1_gate[layer], ffn1_up[layer],
                             ffn1_down[layer])
        x = x + hybrid_mixer(rmsnorm(x, norm_mix[layer]), lb_all[layer], w_in[layer], hg_norm_w[layer],
                             gd_conv_w[layer], gd_a_log[layer], gd_dt_bias[layer], gd_norm_w[layer],
                             rg_conv_w[layer], rg_conv_b[layer], rg_wr[layer], rg_br[layer],
                             rg_wi[layer], rg_bi[layer], rg_lambda[layer], w_out[layer])
        x = x + 0.5 * swiglu(rmsnorm(x, norm_ffn2[layer]), ffn2_gate[layer], ffn2_up[layer],
                             ffn2_down[layer])
    return rmsnorm(x, norm_final)


DEPTH_2 = 1

PLE_DIM = 256
RET_HEADS = 4
RET_QK_DIM = 256
RET_V_DIM = 512
RET_CHUNK = 128
RET_ROPE_BASE = 10000.0
DIL_GROUPS = ((128, 1), (512, 4), (2048, 16))
DIL_SLOTS = 8
DIL_HEAD_DIM = 64
DIL_BLOCK = 128
ROPE_THETA = 500000.0
ROPE_DIM = DIL_HEAD_DIM // 4
D_FF_2 = 4 * D_MODEL

RET_QK_W = RET_HEADS * RET_QK_DIM
RET_V_W = RET_HEADS * RET_V_DIM
DIL_HEADS = len(DIL_GROUPS) * DIL_SLOTS
DIL_W = DIL_HEADS * DIL_HEAD_DIM
DIL_OUT_W = DIL_SLOTS * DIL_HEAD_DIM
SPLITS = (RET_QK_W, RET_QK_W, RET_V_W, RET_V_W, DIL_W, DIL_W, DIL_W, D_MODEL, D_MODEL)
IN_W = RET_QK_W * 2 + RET_V_W * 2 + DIL_W * 3 + D_MODEL * 2


def rmsnorm_2(x, g=None):
    xf = x.astype(jnp.float32)
    y = xf * lax.rsqrt(jnp.mean(xf * xf, axis=-1, keepdims=True) + EPS)
    if g is not None:
        y = y * g.astype(jnp.float32)
    return y.astype(x.dtype)

def rope(x, cos, sin, rot_dim):
    half = rot_dim // 2
    x1 = x[..., :half]
    x2 = x[..., half:rot_dim]
    return jnp.concatenate([x1 * cos - x2 * sin, x2 * cos + x1 * sin, x[..., rot_dim:]], axis=-1)

def retention(q, k, v, pos):
    B, S, H, dk = q.shape
    dv = v.shape[-1]
    f32 = jnp.float32
    half = dk // 2
    inv_freq = 1.0 / (RET_ROPE_BASE ** jnp.linspace(0.0, 1.0, half, dtype=f32))
    ang = pos.astype(f32)[:, :, None, None] * inv_freq
    cos, sin = jnp.cos(ang), jnp.sin(ang)
    q = rope(q.astype(f32), cos, sin, dk)
    k = rope(k.astype(f32), cos, sin, dk) * (dk ** -0.5)
    v = v.astype(f32)
    C = RET_CHUNK
    Sp = -(-S // C) * C
    padw = ((0, 0), (0, Sp - S), (0, 0), (0, 0))
    nc = Sp // C
    qc = jnp.pad(q, padw).reshape(B, nc, C, H, dk)
    kc = jnp.pad(k, padw).reshape(B, nc, C, H, dk)
    vc = jnp.pad(v, padw).reshape(B, nc, C, H, dv)
    log_gamma = jnp.log1p(-(2.0 ** (-5.0 - jnp.arange(H, dtype=f32))))
    idx = jnp.arange(C, dtype=f32)
    diff = idx[:, None] - idx[None, :]
    decay = jnp.where(diff[None] >= 0, jnp.exp(jnp.maximum(diff, 0.0)[None] * log_gamma[:, None, None]), 0.0)
    scores = jnp.einsum('bnihd,bnjhd->bnhij', qc, kc) * decay[None, None]
    inner = jnp.einsum('bnhij,bnjhe->bnihe', scores, vc)
    q_dec = jnp.exp((idx + 1.0)[:, None] * log_gamma[None, :])
    k_dec = jnp.exp((C - 1.0 - idx)[:, None] * log_gamma[None, :])
    chunk_dec = jnp.exp(C * log_gamma)

    def step(R, inp):
        qn, kn, vn = inp
        cross = jnp.einsum('bihd,bhde->bihe', qn * q_dec[None, :, :, None], R)
        R = R * chunk_dec[None, :, None, None] + jnp.einsum('bjhd,bjhe->bhde', kn * k_dec[None, :, :, None], vn)
        return R, cross

    R0 = jnp.zeros((B, H, dk, dv), f32)
    _, cross = lax.scan(step, R0, (jnp.moveaxis(qc, 1, 0), jnp.moveaxis(kc, 1, 0), jnp.moveaxis(vc, 1, 0)))
    y = inner + jnp.moveaxis(cross, 0, 1)
    return y.reshape(B, Sp, H, dv)[:, :S]

def dilated_group(q, k, v, window, dilation):
    B, S, Hg, hd = q.shape
    f32 = jnp.float32
    band = window // dilation
    QB = DIL_BLOCK
    seg = dilation * QB
    Sp = -(-S // seg) * seg
    L = Sp // dilation
    nb = L // QB
    padw = ((0, 0), (0, Sp - S), (0, 0), (0, 0))

    def to_streams(t):
        t = jnp.pad(t.astype(f32), padw).reshape(B, L, dilation, Hg, hd)
        return t.transpose(0, 2, 1, 3, 4).reshape(B, dilation, nb, QB, Hg, hd)

    def with_prev(t):
        prev = jnp.pad(t[:, :, :-1], ((0, 0), (0, 0), (1, 0), (0, 0), (0, 0), (0, 0)))
        return jnp.concatenate([prev, t], axis=3)

    qs = to_streams(q)
    kk = with_prev(to_streams(k))
    vv = with_prev(to_streams(v))
    s = jnp.einsum('bcnqhe,bcnkhe->bcnhqk', qs, kk) * (hd ** -0.5)
    qi = jnp.arange(QB)[:, None]
    kj = jnp.arange(2 * QB)[None, :] - QB
    dist = qi - kj
    in_band = (dist >= 0) & (dist <= band)
    key_exists = (jnp.arange(nb)[:, None, None] * QB + kj[None]) >= 0
    mask = in_band[None] & key_exists
    s = jnp.where(mask[None, None, :, None], s, -1e30)
    lse = jax.nn.logsumexp(s, axis=-1)
    pr = jnp.exp(s - lse[..., None])
    o = jnp.einsum('bcnhqk,bcnkhe->bcnqhe', pr, vv)
    o = o.reshape(B, dilation, L, Hg, hd).transpose(0, 2, 1, 3, 4).reshape(B, Sp, Hg, hd)[:, :S]
    lse = lse.transpose(0, 1, 2, 4, 3).reshape(B, dilation, L, Hg).transpose(0, 2, 1, 3).reshape(B, Sp, Hg)[:, :S]
    return o, lse

def dilated_attention(q, k, v, pos):
    f32 = jnp.float32
    freqs = ROPE_THETA ** (-jnp.arange(0, ROPE_DIM, 2, dtype=f32) / ROPE_DIM)
    ang = pos.astype(f32)[:, :, None, None] * freqs
    cos, sin = jnp.cos(ang), jnp.sin(ang)
    q = rope(q.astype(f32), cos, sin, ROPE_DIM)
    k = rope(k.astype(f32), cos, sin, ROPE_DIM)
    outs, lses = [], []
    for g, (window, dilation) in enumerate(DIL_GROUPS):
        sl = slice(g * DIL_SLOTS, (g + 1) * DIL_SLOTS)
        o, l = dilated_group(q[:, :, sl], k[:, :, sl], v[:, :, sl], window, dilation)
        outs.append(o)
        lses.append(l)
    w = jax.nn.softmax(jnp.stack(lses, axis=0), axis=0)
    return jnp.sum(w[..., None] * jnp.stack(outs, axis=0), axis=0)

def second_inputs(seed: int = 0) -> dict:
    key = jax.random.key(seed)
    ks = jax.random.split(key, 24)
    f32 = jnp.float32
    nrm = lambda k, shape, fan_in: jax.random.normal(k, shape, f32) * (fan_in ** -0.5)
    gain = lambda k: 1.0 + 0.02 * jax.random.normal(k, (DEPTH_2, D_MODEL), f32)
    x = jax.random.normal(ks[0], (BATCH, SEQ, D_MODEL), f32)
    p = jax.random.normal(ks[1], (DEPTH_2, BATCH, SEQ, PLE_DIM), f32)
    positions = jnp.broadcast_to(jnp.arange(SEQ, dtype=jnp.int32)[None, :], (BATCH, SEQ))
    return {
        "x": x,
        "p": p,
        "positions": positions,
        "w_in": nrm(ks[2], (DEPTH_2, D_MODEL, IN_W), D_MODEL),
        "b_gate": 0.01 * jax.random.normal(ks[3], (DEPTH_2, 2, D_MODEL), f32),
        "w_ret_out": nrm(ks[4], (DEPTH_2, RET_V_W, D_MODEL), RET_V_W),
        "w_dil_out": nrm(ks[5], (DEPTH_2, DIL_OUT_W, D_MODEL), DIL_OUT_W),
        "w_o": nrm(ks[6], (DEPTH_2, D_MODEL, D_MODEL), D_MODEL),
        "g_pre_mix": gain(ks[7]),
        "g_post_mix": gain(ks[8]),
        "g_pre_mlp": gain(ks[9]),
        "g_post_mlp": gain(ks[10]),
        "w_up": nrm(ks[11], (DEPTH_2, D_MODEL, D_FF_2), D_MODEL),
        "w_down": nrm(ks[12], (DEPTH_2, D_FF_2, D_MODEL), D_FF_2),
        "g_pre_ple": gain(ks[13]),
        "w_ple_gate": nrm(ks[14], (DEPTH_2, D_MODEL, D_MODEL), D_MODEL),
        "b_ple_gate": 0.01 * jax.random.normal(ks[15], (DEPTH_2, D_MODEL), f32),
        "w_ple_in": nrm(ks[16], (DEPTH_2, PLE_DIM, D_MODEL), PLE_DIM),
        "g_post_ple": gain(ks[17]),
    }

def second_block(x, p, positions, w_in, b_gate, w_ret_out, w_dil_out, w_o, g_pre_mix, g_post_mix,
              g_pre_mlp, g_post_mlp, w_up, w_down, g_pre_ple, w_ple_gate, b_ple_gate, w_ple_in,
              g_post_ple):
    B, S, _ = x.shape
    split_points = [int(s) for s in np.cumsum(SPLITS)[:-1]]
    h = x
    for i in range(DEPTH_2):
        u = rmsnorm_2(h, g_pre_mix[i])
        proj = u @ w_in[i]
        rq, rk, rv, rg, aq, ak, av, gr, ga = jnp.split(proj, split_points, axis=-1)
        yr = retention(rq.reshape(B, S, RET_HEADS, RET_QK_DIM), rk.reshape(B, S, RET_HEADS, RET_QK_DIM),
                       rv.reshape(B, S, RET_HEADS, RET_V_DIM), positions)
        yr = rmsnorm_2(yr) * jax.nn.silu(rg.reshape(B, S, RET_HEADS, RET_V_DIM).astype(jnp.float32))
        ya_branch = yr.reshape(B, S, RET_V_W).astype(h.dtype) @ w_ret_out[i]
        ya = dilated_attention(aq.reshape(B, S, DIL_HEADS, DIL_HEAD_DIM), ak.reshape(B, S, DIL_HEADS, DIL_HEAD_DIM),
                               av.reshape(B, S, DIL_HEADS, DIL_HEAD_DIM), positions)
        yb_branch = ya.reshape(B, S, DIL_OUT_W).astype(h.dtype) @ w_dil_out[i]
        mixed = jax.nn.sigmoid(gr + b_gate[i, 0]) * ya_branch + jax.nn.sigmoid(ga + b_gate[i, 1]) * yb_branch
        h = h + rmsnorm_2(mixed @ w_o[i], g_post_mix[i])
        v2 = rmsnorm_2(h, g_pre_mlp[i])
        f = jnp.square(jax.nn.relu(v2 @ w_up[i])) @ w_down[i]
        h = h + rmsnorm_2(f, g_post_mlp[i])
        gate = jax.nn.sigmoid(rmsnorm_2(h, g_pre_ple[i]) @ w_ple_gate[i] + b_ple_gate[i])
        e = p[i].astype(h.dtype) @ w_ple_in[i]
        h = h + rmsnorm_2(gate * e, g_post_ple[i])
    return h


def setup_inputs(seed=0):
    out = dict(first_inputs(seed))
    for name, value in second_inputs(seed + 1).items():
        if name != "x":
            out[name + "_2"] = value
    return out


def reference(
    x, norm_ffn1, ffn1_gate, ffn1_up, ffn1_down, norm_mix, w_in, hg_lb, hg_norm_w, gd_conv_w,
    gd_a_log, gd_dt_bias, gd_norm_w, rg_conv_w, rg_conv_b, rg_wr, rg_br, rg_wi, rg_bi,
    rg_lambda, w_out, norm_ffn2, ffn2_gate, ffn2_up, ffn2_down, norm_final, p_2, positions_2,
    w_in_2, b_gate_2, w_ret_out_2, w_dil_out_2, w_o_2, g_pre_mix_2, g_post_mix_2, g_pre_mlp_2,
    g_post_mlp_2, w_up_2, w_down_2, g_pre_ple_2, w_ple_gate_2, b_ple_gate_2, w_ple_in_2,
    g_post_ple_2,
):
    x = first_block(
        x, norm_ffn1, ffn1_gate, ffn1_up, ffn1_down, norm_mix, w_in, hg_lb, hg_norm_w,
        gd_conv_w, gd_a_log, gd_dt_bias, gd_norm_w, rg_conv_w, rg_conv_b, rg_wr, rg_br, rg_wi,
        rg_bi, rg_lambda, w_out, norm_ffn2, ffn2_gate, ffn2_up, ffn2_down, norm_final,
    )
    return second_block(
        x, p_2, positions_2, w_in_2, b_gate_2, w_ret_out_2, w_dil_out_2, w_o_2, g_pre_mix_2,
        g_post_mix_2, g_pre_mlp_2, g_post_mlp_2, w_up_2, w_down_2, g_pre_ple_2, w_ple_gate_2,
        b_ple_gate_2, w_ple_in_2, g_post_ple_2,
    )


_drawn_inputs = setup_inputs


def setup_inputs(seed=0):
    import zlib

    import numpy as np

    out = dict(_drawn_inputs(seed))
    spreads = {}
    factors = {'hg_norm_w': 4.696,
     'gd_norm_w': 3.373,
     'rg_br': 6.645,
     'rg_bi': 4.56,
     'norm_ffn2': 3.65,
     'b_gate_2': 8.0,
     'g_post_mix_2': 4.082,
     'g_pre_mlp_2': 12.963,
     'g_post_mlp_2': 19.656,
     'g_pre_ple_2': 33.549,
     'b_ple_gate_2': 64.0,
     'g_post_ple_2': 25.806}
    for name, (base, spread) in spreads.items():
        noise = np.random.default_rng([zlib.crc32(name.encode()), seed]).standard_normal(out[name].shape)
        drawn = base * np.exp(spread * noise) if base else spread * noise
        out[name] = jnp.asarray(drawn.astype(out[name].dtype))
    for name, factor in factors.items():
        out[name] = (out[name] * factor).astype(out[name].dtype)
    return out
```

```python
from contextlib import ExitStack

import numpy as np

import concourse.bass as bass
from concourse import mybir

ALU = mybir.AluOpType
ACT = mybir.ActivationFunctionType
AX = mybir.AxisListType
F32 = mybir.dt.float32
F32R = mybir.dt.float32r
I32 = mybir.dt.int32

P = 128
T = 256
NT = T // P
D = 1024
KD = D // P
DEPTH = 2
D_FF = 2816
PC = 256
PANEL = KD * PC
EPS = 1e-6
LEVELS = [64, 32, 16, 8, 4, 2, 1]
HG_H, HG_D = 4, 64
GD_H, GD_D = 4, 128
GATES0 = 4 * 256 + 4 * 512
RGX0 = GATES0 + 2 * GD_H
RET_H, RET_QK, RET_V = 4, 256, 512
DIL_G, DIL_S, DIL_D = 3, 8, 64
DIL_HALF = DIL_D // 4 // 2
RAW_SLOTS, SPLIT_SLOTS, OP_SLOTS = 3, 2, 4

COLS = [("norm_ffn1", 16), ("norm_mix", 16), ("norm_ffn2", 16), ("norm_final", 8), ("g_pre_mix_2", 8),
        ("g_post_mix_2", 8), ("g_pre_mlp_2", 8), ("g_post_mlp_2", 8), ("g_pre_ple_2", 8),
        ("g_post_ple_2", 8), ("b_gate_2", 16), ("b_ple_gate_2", 8), ("hg_lb", 4), ("hg_norm_w", 2),
        ("gd_norm_w", 2), ("gd_conv_w", 96), ("rg_conv_w", 16), ("rg_conv_b", 4), ("rg_br", 4),
        ("rg_bi", 4), ("rg_lambda", 4), ("dt_rows", 2), ("a_log_rows", 2)]
COL_AT = {}
NCOL = 0
for _name, _n in COLS:
    COL_AT[_name] = NCOL
    NCOL += _n

CONSTS = [("ident", P), ("ones", P), ("head_ones", P), ("masks", len(LEVELS) * P), ("neg", P),
          ("sel", 8 * P), ("sel_beta", 1), ("sel_g", 1), ("inv_freq", 1), ("freqs", DIL_HALF)]
CONST_AT = {}
NCONST = 0
for _name, _n in CONSTS:
    CONST_AT[_name] = NCONST
    NCONST += _n
N_DECAY = RET_H * 3 * P
N_DIL = DIL_G * 3 * P


def shape_constants():
    f = np.float32
    c = np.zeros((P, NCONST), f)

    def put(name, a):
        c[:, CONST_AT[name]:CONST_AT[name] + a.shape[1]] = a

    s, t = np.arange(P)[:, None], np.arange(P)[None, :]
    put("ident", (s == t).astype(f))
    put("ones", np.ones((P, P), f))
    put("head_ones", (s // HG_D == t // HG_D).astype(f))
    put("masks", np.concatenate([((s // (2 * n) == t // (2 * n)) & (s // n < t // n)).astype(f) for n in LEVELS], 1))
    put("neg", np.where(s <= t, 0, -1e30).astype(f))
    sel = np.zeros((P, 8, P), f)
    for i in range(8):
        sel[i, i] = 1
    put("sel", sel.reshape(P, -1))
    rows = np.arange(P)[:, None]
    put("sel_beta", (rows < GD_H).astype(f))
    put("sel_g", ((rows >= GD_H) & (rows < 2 * GD_H)).astype(f))
    put("inv_freq", (f(1) / f(10000) ** np.linspace(0, 1, P, dtype=f))[:, None].astype(f))
    put("freqs", np.broadcast_to(f(500000) ** (-np.arange(0, 2 * DIL_HALF, 2, dtype=f) / f(2 * DIL_HALF)), (P, DIL_HALF)))
    decay = np.zeros((P, RET_H, 3, P), np.float64)
    for h in range(RET_H):
        g = np.log1p(-(2.0 ** (-5.0 - h)))
        for b, shift in enumerate((0, P, 0)):
            dist = t - s + shift
            decay[:, h, b] = np.where(dist >= 0, np.exp(np.maximum(dist, 0) * g), 0) * RET_QK ** -0.5
    q = np.arange(P)[:, None]
    parts = []
    for j in range(2):
        for window, dil in ((128, 1), (512, 4), (2048, 16)):
            dist = q + j * P - np.arange((j + 1) * P)[None, :]
            ok = (dist >= 0) & (dist % dil == 0) & (dist // dil <= window // dil)
            parts.append(np.where(ok, 0, -1e30))
    return c, decay.reshape(P, -1).astype(f), np.concatenate(parts, 1).astype(f)


def build(nc, ap, out, stop_at=None):
    ctx = ExitStack()
    with ctx:
        def sb(name, shape, dt=F32):
            return ctx.enter_context(nc.sbuf_tensor(name, shape, dt))

        sems = {}

        def sem(name):
            if name not in sems:
                sems[name] = ctx.enter_context(nc.semaphore(name))
            return sems[name]

        raw = sb("raw", [P, RAW_SLOTS, PANEL])
        w_hi = sb("w_hi", [P, SPLIT_SLOTS, PANEL], F32R)
        w_lo = sb("w_lo", [P, SPLIT_SLOTS, PANEL], F32R)
        u_hi = sb("u_hi", [P, KD, T], F32R)
        u_lo = sb("u_lo", [P, KD, T], F32R)
        op_hi = sb("op_hi", [P, OP_SLOTS, 2 * T], F32R)
        op_lo = sb("op_lo", [P, OP_SLOTS, 2 * T], F32R)
        x = sb("x", [P, KD, T])
        u32 = sb("u32", [P, KD, T])
        sq = sb("sq", [P, KD, T])
        act_t = sb("act_t", [P, 2, 2 * T])
        hid = sb("hid", [P, 2, 2 * T])
        rstd = sb("rstd", [P, T])
        lnv = sb("lnv", [P, T])
        cols = sb("cols", [P, NCOL])
        cst = sb("cst", [P, NCONST])
        rg_w = sb("rg_w_sb", [P, DEPTH * 4 * P])
        gates_c = sb("gates_c", [8, T])
        small = sb("small", [P, 160])
        bias = sb("bias", [P, 3])
        arena = sb("arena", [P, 17450])
        acc = ctx.enter_context(nc.psum_tensor("acc", [P, KD * T], F32))
        colb = ctx.enter_context(nc.psum_tensor("colb", [P, 3, 2 * T], F32))
        aux = ctx.enter_context(nc.psum_tensor("aux", [P, 2 * T], F32))
        bank = [acc[:, 512 * i:512 * i + 512] for i in range(4)]

        def c(name, i=0, n=1, rows=P):
            o = COL_AT[name] + i
            return cols[0:rows, o:o + n]

        def k(name, i=0, n=1, rows=P):
            o = CONST_AT[name] + i
            return cst[0:rows, o:o + n]

        ident, ones, head_ones = k("ident", 0, P), k("ones", 0, P), k("head_ones", 0, P)
        bias_eps, bias_lndk, bias_hpi = bias[:, 0:1], bias[:, 1:2], bias[:, 2:3]

        def view(at, *shape):
            n = int(np.prod(shape))
            v = arena[:, at:at + n]
            if len(shape) == 2:
                v = v.rearrange("p (a b) -> p a b", b=shape[1])
            if len(shape) == 3:
                v = v.rearrange("p (a b c) -> p a b c", b=shape[1], c=shape[2])
            return v

        def bc(v, axis, n):
            s = list(v.shape)
            s.insert(axis, n)
            return v.unsqueeze(axis).broadcast_to(s)

        z = view(0, 4, T)
        qkv = view(1024, 12, T)
        F0, T0 = 4096, 4096 + 6186
        gd_in = view(F0, 12, T + 3)
        rg_in = view(F0 + 3108, 2, T + 3)
        hf = view(F0 + 3626, 2, T)
        hq = view(F0 + 4138, 2, T)
        hgate = view(F0 + 4650, 2, T)
        hv = view(F0 + 5162, NT, T)
        rgate = view(F0 + 5674, 2, T)
        xc, r_ig = view(T0, 2, T), view(T0 + 512, 4, T)
        rt, rrcp, rsq = view(T0 + 1536, 2, T), view(T0 + 2048, 2, T), view(T0 + 2560, 2, T)
        ra, rbx, rh = view(T0 + 3072, 2, T), view(T0 + 3584, 2, T), view(T0 + 4096, 2, T)
        gt = [arena[0:8, T0 + 4608 + T * i:T0 + 4608 + T * i + T] for i in range(10)]
        hk, hcum = view(T0, 2, T), view(T0 + 512, 2, T)
        de = view(T0 + 1024, 8, 2 * T)
        hat = view(T0 + 5120, 2, 4, P)
        hax = view(T0 + 6144, 2, 2 * P)
        ho = view(T0 + 6656, 2, T)
        G0 = F0
        rbeta, dt_, eq = view(G0, 4, T), view(G0 + 1024, 2, 4 * P), view(G0 + 2048, 4, P)
        lt, sc = view(G0 + 2560, 2, 4 * P), view(G0 + 3584, 2, 4 * P)
        xi, xt = view(G0 + 4608, 2, 4 * P), view(G0 + 5632, 2, 4 * P)
        ntm, yl = view(G0 + 6656, 2, 4 * P), view(G0 + 7680, 2, 4 * P)
        vtok, ktok = view(G0 + 8704, 2, 4 * P), view(G0 + 9728, 4, P)
        vn = view(G0 + 10240, 2, 4 * P)
        rr, vs = view(G0 + 6656, 4, P), view(G0 + 7168, 4, P)
        st, tmp = view(G0 + 7680, 4, P), view(G0 + 8192, 4, P)
        go, grs = view(G0 + 4608, 4, T), view(G0 + 2560, 4, T)
        gcol = small[:, 0:16]
        gexp = small[:, 16:20]
        sp4 = small[:, 20:24]
        lbv, omlb = small[:, 24:28], small[:, 28:32]
        neg_a = small[0:8, 32:34]

        rqk = view(0, 16, T)
        rv = view(4096, NT, RET_H * RET_V)
        rg = view(8192, 16, T)
        rp = view(12288, 2, 3 * P)
        ry = view(13056, 4, T)
        dec = view(14080, RET_H, 3 * P)
        csin, ccos = view(15616, 2, T)[:, 0, :], view(15616, 2, T)[:, 1, :]
        posf = view(16128, 1, T)[:, 0, :]
        angt = view(16384, 4, T)
        qt, kt_ = view(0, 12, T), view(3072, 12, T)
        av = view(6144, NT, DIL_G * DIL_S * DIL_D)
        dtok = view(9216, 2, 2 * T)
        ds_, dp = view(10240, 1, 9 * P)[:, 0, :], view(11392, 1, 9 * P)[:, 0, :]
        do = view(12544, NT, DIL_S * DIL_D)
        ya = view(13568, KD, T)
        dmask = view(15616, 1, N_DIL)[:, 0, :]
        dcs = view(16768, 2, NT * DIL_HALF)
        dang = view(16800, 4, NT * DIL_HALF)
        drop = view(16864, 4, NT * 4 * DIL_HALF)[:, :, 0:NT * 4 * DIL_HALF]
        sga = view(0, KD, T)
        gate_t = view(2048, KD, T)
        p32 = view(6144, 2, T)
        posc = small[:, 40:42]
        dmax = small[:, 48:64]
        drow = small[:, 64:80]
        drinv = small[:, 80:96]
        dneg = small[:, 96:112]

        schedule, panels, ops = [], [], []
        n_col = n_act = n_dve = n_row = 0
        count = {"norm": 0, "fill": 0, "x": 0, "u32": 0, "normed": 0}
        acc_reader = [None]

        def panel(src, kt, ncols, kind, xop, ready, **more):
            nonlocal n_col, n_act, n_dve, n_row
            r = dict(p=len(panels), src=src, kt=kt, nc=ncols, kind=kind, xop=xop, ready=ready, **more)
            if kind != "row":
                r["c"] = n_col
                n_col += 1
                if r["by"] == "act":
                    n_act += 1
                    r["n"] = n_act
                else:
                    n_dve += 1
                    r["n"] = n_dve
            else:
                n_row += 1
            panels.append(r)
            schedule.append(("panel", r))
            return r

        def step(name, **more):
            schedule.append((name, dict(panel=len(panels), nx=count["x"], op=len(ops), **more)))

        def u_op(kk):
            return u_hi[:, kk, :], u_lo[:, kk, :]

        def fill(src_kind, **more):
            count["fill"] += 1
            step("fill", n=count["fill"], src=src_kind, u32=count["u32"], **more)
            count["u32"] += 4 if src_kind == "norm" else 1
            return count["fill"]

        def norm_sum(src):
            count["norm"] += 1
            step("norm_sum", n=count["norm"], src=src, x=count["x"])
            return count["norm"]

        def pre_norm(gain, at):
            n = norm_sum("x")
            return fill("norm", gain=gain, at=at, norm=n)

        def x_update(kind, **more):
            count["x"] += 1
            step("x_update", kind=kind, **more)
            if kind in ("half", "whole"):
                acc_reader[0] = ("x_updated", count["x"])
            if kind == "post":
                count["normed"] += 1
                acc_reader[0] = ("acc_normed", count["normed"])

        def operand(src, ready):
            r = dict(r=len(ops), src=src, ready=ready)
            ops.append(r)
            return r

        def op_tiles(r):
            def get(kk):
                s = r["r"] % OP_SLOTS
                return op_hi[:, s, T * kk:T * kk + T], op_lo[:, s, T * kk:T * kk + T]
            return get

        def kpn(w):
            return w.rearrange("(k p) n -> p k n", p=P)

        def row_gemm_panel(w, i, r, first, last, base=None):
            if r is not None:
                ready = [("op_ready", r["r"] + 1)]
                r["panel"] = len(panels)
                get = op_tiles(r)
            else:
                ready = base[0]
                get = (lambda kk, i=i: base[1](2 * i + kk))
            if first and acc_reader[0]:
                ready = ready + [acc_reader[0]]
            panel(kpn(w)[:, 2 * i:2 * i + 2, :], 2, D, "row", get, ready, first=first, last=last)

        def ffn(layer, gain, gate, up, down):
            f = pre_norm(gain, KD * layer)
            n = D_FF // PC
            todo = None
            for i in range(n):
                g = panel(kpn(gate)[:, :, i * PC:(i + 1) * PC], KD, PC, "A", u_op, [("u_ready", 4 * f)],
                          by="act", evac=("silu_h", len(ops)))
                if i:
                    step("op_lo", r=todo)
                u = panel(kpn(up)[:, :, i * PC:(i + 1) * PC], KD, PC, "A", u_op, [], by="dve",
                          evac=("h", len(ops), g["n"]))
                r = operand(hid[:, len(ops) % 2, :], [("dve_evac", u["n"])])
                step("op_hi", r=r)
                if i:
                    row_gemm_panel(down, i - 1, todo, i == 1, False)
                todo = r
            step("op_lo", r=todo)
            row_gemm_panel(down, n - 1, todo, n == 1, True)
            x_update("half")

        def mixer(l):
            f = pre_norm("norm_mix", KD * l)
            w = kpn(ap["w_in"][l])
            ready = [("u_ready", 4 * f)]

            def cp(c0, n, kind, evac, by="act"):
                return panel(w[:, :, c0:c0 + n], KD, n, kind, u_op, ready, by=by, evac=evac)["n"]

            g = cp(GATES0, P, "A", ("copy", gt[0], 0, 8), by="dve")
            for i in range(6):
                a = cp(1024 + i * PC, PC, "A", ("copy", gd_in[:, 2 * i:2 * i + 2, 3:], 0))
            b = cp(RGX0, PC, "A", ("copy", rg_in[:, :, 3:], 0))
            d = cp(RGX0 + PC, PC, "A", ("gelu", rgate))
            cp(256, PC, "A", ("sigmoid", hf))
            cp(0, PC, "A", ("silu", hq))
            cp(768, PC, "A", ("silu", hgate))
            for i in range(2):
                cp(2560 + i * PC, PC, "A", ("silu", z[:, 2 * i:2 * i + 2, :]))
            e = cp(512, PC, "B", ("copy", hv, 0))
            kw = dict(l=l, evac=e)
            for s in ("gates", "rg", "hg", "gd"):
                step(s, **kw)
            f = fill("y")
            for i in range(4):
                row_gemm_panel(ap["w_out"][l], i, None, i == 0, i == 3, ([("u_ready", 4 * f)], u_op))
            x_update("whole")

        for l in range(DEPTH):
            ffn(l, "norm_ffn1", ap["ffn1_gate"][l], ap["ffn1_up"][l], ap["ffn1_down"][l])
            if stop_at == "ffn1":
                break
            mixer(l)
            if stop_at == "mix":
                break
            ffn(l, "norm_ffn2", ap["ffn2_gate"][l], ap["ffn2_up"][l], ap["ffn2_down"][l])
            if stop_at == "layer":
                break

        def second_block():
            n = norm_sum("x")
            x_update("final", norm=n)
            if stop_at == "first":
                return
            f = pre_norm("g_pre_mix_2", 0)
            w = kpn(ap["w_in_2"][0])
            ready = [("u_ready", 4 * f)]

            def cp(c0, kind, evac):
                return panel(w[:, :, c0:c0 + PC], KD, PC, kind, u_op, ready, by="act", evac=evac)["n"]

            step("ret_tables")
            for i in range(8):
                e = cp(i * PC, "A", ("copy", rqk[:, 2 * i:2 * i + 2, :], 0))
            step("rope", evac=e)
            for i in range(8):
                e = cp(2048 + i * PC, "B", ("copy", rv[:, :, i * PC:(i + 1) * PC], 0))
            for i in range(8):
                e = cp(4096 + i * PC, "A", ("silu", rg[:, 2 * i:2 * i + 2, :]))
            for h in range(RET_H):
                step("ret_head", h=h, evac=e)
                rs = []
                for i in range(2):
                    r = operand(ry[:, 2 * i:2 * i + 2, :].rearrange("p a b -> p (a b)"), [("ret_y_ready", h + 1)])
                    step("op_hi", r=r)
                    step("op_lo", r=r)
                    rs.append(r)
                for i in range(2):
                    row_gemm_panel(ap["w_ret_out_2"][0], 2 * h + i, rs[i], h + i == 0, (h, i) == (RET_H - 1, 1))
            step("ya")
            acc_reader[0] = ("ya_ready", 1)
            step("dil_tables")
            base = 6144
            for i in range(12):
                step_i = i
                e = cp(base + i * PC, "B", ("copy", dtok[:, i % 2, :].rearrange("p (a b) -> p a b", b=PC), 1))
                step("dil_rope", i=step_i, evac=e)
            for i in range(6):
                e = cp(base + 3072 + i * PC, "B", ("copy", av[:, :, i * PC:(i + 1) * PC], 0))
            step("dil", evac=e)
            for i in range(4):
                r = panel(w[:, :, 10752 + i * PC:10752 + (i + 1) * PC], KD, PC, "A", u_op, [], by="act",
                          evac=("gate_bias", act_t[:, i % 2, :], "b_gate_2", 2 * i, i))
                step("gate_ya", i=i, evac=r["n"])
            for i in range(4):
                e = cp(11776 + i * PC, "A", ("gate_bias", sga[:, 2 * i:2 * i + 2, :], "b_gate_2", KD + 2 * i, None))
            for i in range(2):
                r = operand(("dil_o", i), [("dil_ot", i + 1)])
                step("op_hi", r=r)
                step("op_lo", r=r)
                row_gemm_panel(ap["w_dil_out_2"][0], i, r, i == 0, i == 1)
            step("mixed", evac=e)
            acc_reader[0] = ("acc_mixed", 1)
            f = fill("y")
            for i in range(4):
                row_gemm_panel(ap["w_o_2"][0], i, None, i == 0, i == 3, ([("u_ready", 4 * f)], u_op))
            n = norm_sum("acc")
            x_update("post", norm=n, gain="g_post_mix_2")
            if stop_at == "mix2":
                return
            f = pre_norm("g_pre_mlp_2", 0)
            todo = None
            for i in range(16):
                panel(kpn(ap["w_up_2"][0])[:, :, i * PC:(i + 1) * PC], KD, PC, "A", u_op,
                      [("u_ready", 4 * f)], by="act", evac=("relu", len(ops)))
                step("relu2", r=len(ops), evac=n_act)
                if i:
                    row_gemm_panel(ap["w_down_2"][0], i - 1, todo, i == 1, False)
                r = operand(hid[:, len(ops) % 2, :], [("hid_ready", i + 1)])
                step("op_hi", r=r)
                step("op_lo", r=r)
                todo = r
            row_gemm_panel(ap["w_down_2"][0], 15, todo, False, True)
            n = norm_sum("acc")
            x_update("post", norm=n, gain="g_post_mlp_2")
            if stop_at == "mlp2":
                return
            f = pre_norm("g_pre_ple_2", 0)
            step("load_p")
            r = operand(p32.rearrange("p a b -> p (a b)"), [("p_loaded", 16)])
            step("op_hi", r=r)
            step("op_lo", r=r)
            for i in range(4):
                e = panel(kpn(ap["w_ple_gate_2"][0])[:, :, i * PC:(i + 1) * PC], KD, PC, "A", u_op,
                          [("u_ready", 4 * f)], by="act",
                          evac=("gate_bias", gate_t[:, 2 * i:2 * i + 2, :], "b_ple_gate_2", 2 * i, None))["n"]
            row_gemm_panel(ap["w_ple_in_2"][0], 0, r, True, True)
            step("ple", evac=e)
            n = norm_sum("gated")
            x_update("post_gated", norm=n, gain="g_post_ple_2")

        if stop_at in (None, "first", "mix2", "mlp2"):
            second_block()
        n_x, n_panels = count["x"], len(panels)
        by_column = [r for r in panels if r["kind"] != "row"]

        def split_view(t, r):
            return t[:, r["p"] % SPLIT_SLOTS, 0:r["kt"] * r["nc"]]

        def col_bank_free(eng, n):
            r = by_column[n]
            eng.wait_ge(sem(f"{r['by']}_evac"), r["n"])

        block = ctx.enter_context(nc.Block())

        @block.sync
        def _(sp):
            sp.dma_start(x[:, :, :], ap["x_t"]).then_inc(sem("x_loaded"), 16)
            sp.dma_start(cols[:, :], ap["columns"]).then_inc(sem("cols_loaded"), 16)
            sp.dma_start(cst[:, :], ap["constants"]).then_inc(sem("cst_loaded"), 16)
            sp.dma_start(rg_w[:, :], ap["rg_w"]).then_inc(sem("rg_w_loaded"), 16)
            for what, r in schedule:
                if what == "panel":
                    p = r["p"]
                    if p >= RAW_SLOTS:
                        sp.wait_ge(sem("w_hi_ready"), p - RAW_SLOTS + 1)
                        sp.wait_ge(sem("w_lo_ready"), p - RAW_SLOTS + 1)
                    dst = raw[:, p % RAW_SLOTS, 0:r["kt"] * r["nc"]].rearrange("p (k n) -> p k n", k=r["kt"])
                    sp.dma_start(dst, r["src"]).then_inc(sem(f"raw_loaded{p % RAW_SLOTS}"), 16)
            sp.wait_ge(sem("x_updated"), n_x)
            sp.dma_start(out, x[:, :, :]).then_inc(sem("stored"), 16)
            sp.wait_ge(sem("stored"), 16)

        @block.gpsimd
        def _(pool):
            for what, r in schedule:
                if what == "ret_tables":
                    pool.wait_ge(sem("x_updated"), 7)
                    pool.dma_start(dec.rearrange("p a b -> p (a b)"), ap["decay"]).then_inc(sem("dec_loaded"), 16)
                    pool.dma_start(posf.bitcast(I32), ap["positions"].partition_broadcast(P)).then_inc(sem("pos_loaded"), 16)
                    pool.dma_start(posc.bitcast(I32), ap["positions_c"]).then_inc(sem("posc_loaded"), 16)
                if what == "dil_tables":
                    pool.wait_ge(sem("ya_ready"), 1)
                    pool.dma_start(dmask, ap["dil_mask"]).then_inc(sem("dmask_loaded"), 16)
                if what == "load_p":
                    pool.wait_ge(sem("x_updated"), 9)
                    pool.dma_start(p32, ap["p_t"]).then_inc(sem("p_loaded"), 16)

        @block.tensor
        def _(pe):
            def mm(o, a, b, start=True, stop=True):
                return pe.matmul(o, a, b, start=start, stop=stop, skip_group_check=True)

            def gemm(r):
                p = r["p"]
                for name, v in r["ready"]:
                    pe.wait_ge(sem(name), v)
                if r["kind"] != "row" and r["c"] >= 3:
                    col_bank_free(pe, r["c"] - 3)
                pe.wait_ge(sem("w_hi_ready"), p + 1)
                pe.wait_ge(sem("w_lo_ready"), p + 1)
                wh = split_view(w_hi, r).rearrange("p (k n) -> p k n", k=r["kt"])
                wl = split_view(w_lo, r).rearrange("p (k n) -> p k n", k=r["kt"])
                if r["kind"] == "row":
                    for kk in range(r["kt"]):
                        xh, xl = r["xop"](kk)
                        for m in range(KD):
                            o = acc[:, T * m:T * m + T]
                            m_ = slice(P * m, P * m + P)
                            mm(o, wh[:, kk, m_], xh, r["first"] and kk == 0 and m % 2 == 0, False)
                            mm(o, wh[:, kk, m_], xl, False, False)
                            last = mm(o, wl[:, kk, m_], xh, False, r["last"] and kk == r["kt"] - 1)
                else:
                    for m in range(max(r["nc"] // P, 1)):
                        o = colb[:, r["c"] % 3, T * m:T * m + T]
                        for kk in range(r["kt"]):
                            xh, xl = r["xop"](kk)
                            m_ = slice(P * m, P * m + P)
                            if r["kind"] == "A":
                                trio = ((wh[:, kk, m_], xh), (wh[:, kk, m_], xl), (wl[:, kk, m_], xh))
                            else:
                                trio = ((xh[:, m_], wh[:, kk, :]), (xl[:, m_], wh[:, kk, :]), (xh[:, m_], wl[:, kk, :]))
                            for i, (a, b) in enumerate(trio):
                                last = mm(o, a, b, kk == 0 and i == 0, kk == r["kt"] - 1 and i == 2)
                last.then_inc(sem("panel_used"), 1)

            def norm_sum(r):
                pe.wait_ge(sem("sq_ready"), r["n"])
                for kk in range(KD):
                    last = mm(aux[:, 0:T], ones, sq[:, kk, :], kk == 0, kk == KD - 1)
                last.then_inc(sem("norm_summed"), 1)

            def gates_spread(l):
                pe.wait_ge(sem("gates_ready"), l + 1)
                pe.wait_ge(sem("gd_rn"), l + 1)
                for i in range(8):
                    mm(acc[:, T * i:T * i + T], k("sel", P * i, P, 8), gates_c[:, :])
                for j in range(NT):
                    last = pe.transpose(aux[:, 8 * j:8 * j + 8], gates_c[:, P * j:P * j + P], k("ident", 0, 8, 8))
                last.then_inc(sem("gates_spread"), 1)

            def rg_(r):
                l = r["l"]
                pe.wait_ge(sem("rg_xc"), l + 1)
                for g in range(2):
                    for t in range(2):
                        w = rg_w[:, (l * 4 + g * 2 + t) * P:(l * 4 + g * 2 + t + 1) * P]
                        last = mm(bank[g][:, T * t:T * t + T], w, xc[:, t, :])
                last.then_inc(sem("rg_gates"), 1)

            def hg(r):
                l = r["l"]
                per = 9 * l
                pe.wait_ge(sem("rg_gates_read"), l + 1)
                for i in range(9):
                    if i < 8:
                        pe.wait_ge(sem("hg_qk"), 8 * l + i + 1)
                    if i >= 2:
                        pe.wait_ge(sem("hg_copied"), per + i - 1)
                    for par in range(2):
                        rows = slice(64 * par, 64 * par + 64)
                        b = bank[2 * (i % 2) + par]
                        for ch in range(2):
                            if i == 0:
                                e = de[rows, 0, T * ch:T * ch + T]
                                last = mm(b[:, P * ch:P * ch + P], e[:, 0:P], e[:, P:T])
                                continue
                            for j in range(NT):
                                if i < 8:
                                    e = de[rows, i, T * ch + P * j:T * ch + P * j + P]
                                    a, q = e, e
                                else:
                                    a, q = hk[rows, ch, P * j:P * j + P], hq[rows, ch, P * j:P * j + P]
                                last = mm(b[:, (2 * ch + j) * P:(2 * ch + j + 1) * P], a, q)
                    last.then_inc(sem("hg_scores"), 1)
                pe.wait_ge(sem("hg_copied"), per + 9)
                for par in range(2):
                    for ch in range(2):
                        h = 2 * ch + par
                        o = bank[0][64 * par:64 * par + 64, T * ch:T * ch + T]
                        mm(o[:, 0:P], hv[:, 0, 64 * h:64 * h + 64], hat[:, par, 2 * ch, :])
                        mm(o[:, P:T], hv[:, 0, 64 * h:64 * h + 64], hax[:, par, P * ch:P * ch + P], True, False)
                        last = mm(o[:, P:T], hv[:, 1, 64 * h:64 * h + 64], hat[:, par, 2 * ch + 1, :], False, True)
                last.then_inc(sem("hg_o"), 1)
                pe.wait_ge(sem("hg_sq"), l + 1)
                mm(bank[1], head_ones, sq[:, 0:2, :].rearrange("p a b -> p (a b)")).then_inc(sem("hg_sum"), 1)

            def gd(r):
                l = r["l"]
                pe.wait_ge(sem("gd_sq"), l + 1)
                pe.wait_ge(sem("hg_rstd"), l + 1)
                for i in range(8):
                    last = mm(acc[:, T * i:T * i + T], ones, sq[:, i, :])
                last.then_inc(sem("gd_ss"), 1)
                gates_spread(l)
                for n in range(3):
                    if n:
                        pe.wait_ge(sem("gd_tok"), 3 * l + n)
                    else:
                        pe.wait_ge(sem("gd_qk"), l + 1)
                        pe.wait_ge(sem("gates_read"), l + 1)
                    for h in range(GD_H):
                        src = qkv[:, 8 + h, P * n:P * n + P] if n < 2 else qkv[:, 4 + h, 0:P]
                        last = pe.transpose(aux[:, P * h:P * h + P], src, ident)
                    last.then_inc(sem("gd_turned"), 1)
                for j in range(NT):
                    for h in range(GD_H):
                        kj = qkv[:, 4 + h, P * j:P * j + P]
                        mm(bank[j][:, P * h:P * h + P], kj, kj)
                        last = mm(bank[2 + j][:, P * h:P * h + P], kj, qkv[:, h, P * j:P * j + P])
                last.then_inc(sem("gd_scores"), 1)
                for j in range(NT):
                    pe.wait_ge(sem("gd_x"), 14 * l + j + 1)
                    for h in range(GD_H):
                        last = pe.transpose(bank[j][:, P * h:P * h + P], xt[:, j, P * h:P * h + P], ident)
                    last.then_inc(sem("gd_x0"), 1)
                for i in range(1, 7):
                    for j in range(NT):
                        pe.wait_ge(sem("gd_x"), 14 * l + 2 * i + j + 1)
                        for h in range(GD_H):
                            s = slice(P * h, P * h + P)
                            last = mm(bank[j][:, s], ntm[:, j, s], xi[:, j, s])
                        last.then_inc(sem("gd_y"), 1)
                    for j in range(NT):
                        pe.wait_ge(sem("gd_y_copied"), 12 * l + 2 * (i - 1) + j + 1)
                        for h in range(GD_H):
                            s = slice(P * h, P * h + P)
                            if i < 6:
                                mm(bank[j][:, s], xt[:, j, s], yl[:, j, s])
                            last = mm(bank[2 + j][:, s], yl[:, j, s], xt[:, j, s])
                        last.then_inc(sem("gd_z"), 1)
                hs = [slice(P * h, P * h + P) for h in range(GD_H)]

                def new_values(j, b):
                    pe.wait_ge(sem("gd_r"), 2 * l + j + 1)
                    for h in range(GD_H):
                        last = mm(bank[b][:, hs[h]], xt[:, j, hs[h]], rr[:, h, :])
                    last.then_inc(sem("gd_vn"), 1)

                new_values(0, 0)
                pe.wait_ge(sem("gd_vs"), l + 1)
                for h in range(GD_H):
                    last = mm(bank[1][:, hs[h]], ktok[:, h, :], vs[:, h, :])
                last.then_inc(sem("gd_state"), 1)
                pe.wait_ge(sem("gd_state_copied"), l + 1)
                for h in range(GD_H):
                    last = mm(bank[2][:, hs[h]], qkv[:, 4 + h, P:T], st[:, h, :])
                last.then_inc(sem("gd_ks"), 1)
                new_values(1, 3)
                pe.wait_ge(sem("gd_vn_copied"), l + 1)
                for h in range(GD_H):
                    o = bank[h // 2][:, T * (h % 2):T * (h % 2) + T]
                    mm(o[:, 0:P], vn[:, 0, hs[h]], sc[:, 0, hs[h]])
                    mm(o[:, P:T], vn[:, 1, hs[h]], sc[:, 1, hs[h]], True, False)
                    last = mm(o[:, P:T], st[:, h, :], eq[:, h, :], False, True)
                last.then_inc(sem("gd_o"), 1)
                pe.wait_ge(sem("gd_osq"), l + 1)
                for h in range(GD_H):
                    last = mm(acc[:, 1024 + T * h:1024 + T * h + T], ones, sq[:, h, :])
                last.then_inc(sem("gd_osum"), 1)

            def ret_head(r):
                h = r["h"]
                if h == 0:
                    pe.wait_ge(sem("roped"), 2)
                    pe.wait_ge(sem("act_evac"), r["evac"])
                else:
                    pe.wait_ge(sem("ret_r_ready"), h)
                for s0, n, at in ((0, T, 0), (P, P, T)):
                    for i in range(2):
                        last = mm(aux[:, at:at + n], rqk[:, 8 + 2 * h + i, s0:s0 + P], rqk[:, 2 * h + i, s0:T], i == 0, i == 1)
                last.then_inc(sem("ret_scores"), 1)
                pe.wait_ge(sem("ret_p_ready"), h + 1)
                pr = rp[:, h % 2, :]
                for i in range(4):
                    o = colb[:, i // 2, T * (i % 2):T * (i % 2) + T]
                    e = slice(RET_V * h + P * i, RET_V * h + P * i + P)
                    mm(o, rv[:, 0, e], pr[:, 0:T], True, False)
                    last = mm(o[:, P:T], rv[:, 1, e], pr[:, T:T + P], False, True)
                last.then_inc(sem("ret_y"), 1)
                pe.wait_ge(sem("ret_sq"), h + 1)
                for i in range(4):
                    last = mm(colb[:, 2, 0:T], ones, sq[:, i, :], i == 0, i == 3)
                last.then_inc(sem("ret_sum"), 1)

            def dil_rope(r):
                i = r["i"]
                pe.wait_ge(sem("dil_roped"), i + 1)
                if i:
                    pe.wait_ge(sem("dil_turn_copied"), i)
                d = dtok[:, i % 2, :]
                for j in range(NT):
                    for t in range(2):
                        last = pe.transpose(aux[:, T * t + P * j:T * t + P * j + P], d[:, PC * j + P * t:PC * j + P * t + P], ident)
                last.then_inc(sem("dil_turned"), 1)

            def dil(r):
                pe.wait_ge(sem("dil_turn_copied"), 12)
                pe.wait_ge(sem("act_evac"), r["evac"])
                pe.wait_ge(sem("ya_ready"), 1)
                for a in range(DIL_S):
                    rows = slice(64 * (a % 2), 64 * (a % 2) + 64)
                    if a:
                        pe.wait_ge(sem("dil_masked"), a)
                    for j in range(NT):
                        for g in range(DIL_G):
                            t = 4 * g + a // 2
                            n = P * (j + 1)
                            o = acc[:, 512 * j + n * g:512 * j + n * g + n]
                            last = mm(o, qt[rows, t, P * j:P * j + P], kt_[rows, t, 0:n])
                    last.then_inc(sem("dil_scores"), 1)
                    pe.wait_ge(sem("dil_p"), a + 1)
                    if a:
                        pe.wait_ge(sem("dil_pt"), a)
                    for g in range(DIL_G):
                        for b, at in enumerate((P * g, 3 * P + T * g, 3 * P + T * g + P)):
                            i = 3 * g + b
                            last = pe.transpose(colb[:, i // 4, P * (i % 4):P * (i % 4) + P], ds_[:, at:at + P], ident)
                    last.then_inc(sem("dil_p_turned"), 1)
                    pe.wait_ge(sem("dil_pt"), a + 1)
                    for j in range(NT):
                        o = (bank[3] if j == 0 else aux)[:, 64 * a:64 * a + 64]
                        for g in range(DIL_G):
                            v = slice(64 * (8 * g + a), 64 * (8 * g + a) + 64)
                            for s in range(j + 1):
                                last = mm(o, dp[:, P * (3 * g + j + s):P * (3 * g + j + s + 1)], av[:, s, v],
                                          g == 0 and s == 0, g == DIL_G - 1 and s == j)
                    last.then_inc(sem("dil_pv"), 1)
                pe.wait_ge(sem("dil_o"), 1)
                for t in range(4):
                    for j in range(NT):
                        last = pe.transpose(acc[:, T * t + P * j:T * t + P * j + P], do[:, j, P * t:P * t + P], ident)
                last.then_inc(sem("dil_o_turned"), 1)

            run = {"panel": gemm, "norm_sum": norm_sum, "rg": rg_, "hg": hg, "gd": gd,
                   "ret_head": ret_head, "dil_rope": dil_rope, "dil": dil}
            pe.wait_ge(sem("cst_loaded"), 16)
            pe.wait_ge(sem("rg_w_loaded"), 16)
            for what, r in schedule:
                if what in run:
                    run[what](r)

        @block.scalar
        def _(act):
            chain = [0]

            def link(ins):
                chain[0] += 1
                ins.then_inc(sem("act_chain"), 1)
                act.wait_ge(sem("act_chain"), chain[0])

            def split_hi(r):
                p = r["p"]
                act.wait_ge(sem(f"raw_loaded{p % RAW_SLOTS}"), 16 * (p // RAW_SLOTS + 1))
                if p >= SPLIT_SLOTS:
                    act.wait_ge(sem("panel_used"), p - SPLIT_SLOTS + 1)
                act.activation(split_view(w_hi, r), raw[:, p % RAW_SLOTS, 0:r["kt"] * r["nc"]], ACT.Copy)\
                    .then_inc(sem("w_hi_ready"), 1)

            def act_t_free(n):
                if n >= 2:
                    name, v = ops[n - 2]["ready"][0]
                    act.wait_ge(sem(name), v)

            def panel(r):
                if r["p"] == 0:
                    split_hi(r)
                if r["p"] + 1 < n_panels:
                    split_hi(panels[r["p"] + 1])
                if r["kind"] == "row" or r["by"] != "act":
                    return
                act.wait_ge(sem("panel_used"), r["p"] + 1)
                src = colb[:, r["c"] % 3, :]
                src2 = src.rearrange("p (a b) -> p a b", b=T)
                what = r["evac"]
                if what[0] == "silu_h":
                    act_t_free(what[1])
                    ins = act.activation(act_t[:, what[1] % 2, :], src, ACT.Silu)
                elif what[0] == "relu":
                    act_t_free(what[1])
                    ins = act.activation(act_t[:, what[1] % 2, :], src, ACT.Relu)
                elif what[0] == "gate_bias":
                    if what[4] is not None and what[4] >= 2:
                        act.wait_ge(sem("ya_gated"), what[4] - 1)
                    for m in range(2):
                        dst = what[1] if len(what[1].shape) == 3 else what[1].rearrange("p (a b) -> p a b", b=T)
                        ins = act.activation(dst[:, m, :], src2[:, m, :], ACT.Sigmoid, bias=c(what[2], what[3] + m))
                else:
                    fn = {"copy": ACT.Copy, "gelu": ACT.Gelu_apprx_tanh, "sigmoid": ACT.Sigmoid, "silu": ACT.Silu}[what[0]]
                    if what[0] == "copy" and what[2]:
                        i = r["c"] - first_dil
                        if i >= 2:
                            act.wait_ge(sem("dil_turned"), i - 1)
                    ins = act.activation(what[1], src2, fn)
                ins.then_inc(sem("act_evac"), 1)

            first_dil = next((r["c"] for r in by_column if r["evac"][0] == "copy" and r["evac"][2] == 1), 0)

            def rstd_from(o, s, scale, b2=0.0):
                link(act.activation(o, s, ACT.Ln, bias=bias_eps, scale=scale))
                return act.activation(o, o, ACT.Exp, scale=-0.5, bias=b2)

            def norm_sum(r):
                flat = sq[:, :, :].rearrange("p a b -> p (a b)")
                if r["src"] == "x":
                    if r["x"] == 0:
                        act.wait_ge(sem("x_loaded"), 16)
                    else:
                        act.wait_ge(sem("x_updated"), r["x"])
                    src = x[:, :, :].rearrange("p a b -> p (a b)")
                elif r["src"] == "acc":
                    act.wait_ge(sem("panel_used"), r["panel"])
                    src = acc[:, :]
                else:
                    act.wait_ge(sem("gated_ready"), 1)
                    src = gate_t.rearrange("p a b -> p (a b)")
                act.activation(flat, src, ACT.Square).then_inc(sem("sq_ready"), 1)
                act.wait_ge(sem("norm_summed"), r["n"])
                rstd_from(rstd[:, :], aux[:, 0:T], 1.0 / D).then_inc(sem("rstd_ready"), 1)

            def fill(r):
                act.wait_ge(sem("panel_used"), r["panel"])
                for i in range(4):
                    act.wait_ge(sem("u32_ready"), r["u32"] + (i + 1 if r["src"] == "norm" else 1))
                    act.activation(u_hi[:, 2 * i:2 * i + 2, :], u32[:, 2 * i:2 * i + 2, :], ACT.Copy)\
                        .then_inc(sem("u_hi_ready"), 1)

            def op_hi_(r):
                r = r["r"]
                for name, v in r["ready"]:
                    act.wait_ge(sem(name), v)
                if r["r"] >= OP_SLOTS:
                    act.wait_ge(sem("panel_used"), ops[r["r"] - OP_SLOTS]["panel"] + 1)
                src = r["src"]
                if isinstance(src, tuple):
                    src = u32[:, 2 * src[1]:2 * src[1] + 2, :].rearrange("p a b -> p (a b)")
                act.activation(op_hi[:, r["r"] % OP_SLOTS, :], src, ACT.Copy).then_inc(sem("op_hi_ready"), 1)

            def gates(r):
                l = r["l"]
                act.wait_ge(sem("gates_z"), l + 1)
                act.activation(gt[1], gt[0], ACT.Sigmoid).then_inc(sem("gates_sig"), 1)
                link(act.activation(gt[3], gt[2], ACT.Abs))
                act.activation(gt[4], gt[3], ACT.Exp, scale=-1.0).then_inc(sem("gates_e"), 1)

            def decays(l):
                act.wait_ge(sem("gates_diff"), l + 1)
                act.activation(dt_, dt_, ACT.Exp)
                act.activation(eq, acc[:, 1024:2048].rearrange("p (h t) -> p h t", t=T)[:, :, P:T], ACT.Exp)
                act.activation(gexp, gcol[:, 12:16], ACT.Exp).then_inc(sem("gates_read"), 1)

            def rg_(r):
                l = r["l"]
                act.wait_ge(sem("rg_gates"), l + 1)
                for g in range(2):
                    for t in range(2):
                        ins = act.activation(r_ig[:, 2 * g + t, :], bank[g][:, T * t:T * t + T], ACT.Sigmoid,
                                             bias=c(("rg_br", "rg_bi")[g], 2 * l + t))
                link(ins)
                for t in range(2):
                    ins = act.activation(rt[:, t, :], r_ig[:, t, :], ACT.Tanh, scale=sp4[:, 2 * l + t:2 * l + t + 1])
                ins.then_inc(sem("rg_gates_read"), 1)
                act.wait_ge(sem("rg_tc"), l + 1)
                link(act.activation(rsq, rsq, ACT.Ln))
                act.activation(rsq, rsq, ACT.Exp, scale=0.5).then_inc(sem("rg_root"), 1)

            def hg(r):
                l = r["l"]
                act.wait_ge(sem("hg_f"), l + 1)
                act.activation(hcum, hcum, ACT.Ln).then_inc(sem("hg_logf"), 1)
                act.wait_ge(sem("hg_de"), l + 1)
                act.activation(de, de, ACT.Exp).then_inc(sem("hg_e"), 1)
                act.wait_ge(sem("hg_o"), l + 1)
                link(act.activation(ho, bank[0].rearrange("p (a b) -> p a b", b=T), ACT.Copy))
                act.activation(sq[:, 0:2, :], ho, ACT.Square).then_inc(sem("hg_sq"), 1)
                act.wait_ge(sem("hg_sum"), l + 1)
                rstd_from(act_t[:, 0, :], bank[1], 1.0 / HG_D).then_inc(sem("hg_rstd"), 1)

            def gd(r):
                l = r["l"]
                act.wait_ge(sem("gd_conv"), l + 1)
                link(act.activation(qkv, qkv, ACT.Silu))
                act.wait_ge(sem("hg_sum"), l + 1)
                act.activation(sq[:, :, :], qkv[:, 0:8, :], ACT.Square).then_inc(sem("gd_sq"), 1)
                act.wait_ge(sem("gd_ss"), l + 1)
                flat = sq[:, :, :].rearrange("p a b -> p (a b)")
                link(act.activation(flat, acc[:, :], ACT.Ln, bias=bias_eps))
                act.activation(flat[:, 0:1024], flat[:, 0:1024], ACT.Exp, scale=-0.5, bias=bias_lndk)
                act.activation(flat[:, 1024:2048], flat[:, 1024:2048], ACT.Exp, scale=-0.5).then_inc(sem("gd_rn"), 1)
                decays(l)
                for n in range(3):
                    act.wait_ge(sem("gd_turned"), 3 * l + n + 1)
                    dst = vtok[:, n, :] if n < 2 else ktok.rearrange("p a b -> p (a b)")
                    act.activation(dst, aux[:, :], ACT.Copy).then_inc(sem("gd_tok"), 1)
                for i in range(6):
                    for j in range(NT):
                        act.wait_ge(sem("gd_y"), 12 * l + 2 * i + j + 1)
                        act.activation(yl[:, j, :], bank[j], ACT.Copy).then_inc(sem("gd_y_copied"), 1)
                act.wait_ge(sem("gd_state"), l + 1)
                act.activation(st.rearrange("p a b -> p (a b)"), bank[1], ACT.Copy).then_inc(sem("gd_state_copied"), 1)
                act.wait_ge(sem("gd_o"), l + 1)
                link(act.activation(go.rearrange("p a b -> p (a b)"), acc[:, 0:1024], ACT.Copy))
                act.activation(sq[:, 0:4, :], go, ACT.Square).then_inc(sem("gd_osq"), 1)
                act.wait_ge(sem("gd_osum"), l + 1)
                rstd_from(grs.rearrange("p a b -> p (a b)"), acc[:, 1024:2048], 1.0 / GD_D).then_inc(sem("gd_orstd"), 1)

            def ret_tables(r):
                act.wait_ge(sem("ret_angles"), 1)
                act.activation(csin, angt[:, 0, :], ACT.Sin)
                act.activation(ccos, angt[:, 1, :], ACT.Sin).then_inc(sem("ret_sincos"), 1)

            def ret_head(r):
                h = r["h"]
                act.wait_ge(sem("ret_y"), h + 1)
                if h:
                    act.wait_ge(sem("op_ready"), r["op"])
                link(act.activation(ry.rearrange("p a b -> p (a b)"), colb[:, 0:2, :].rearrange("p a b -> p (a b)"), ACT.Copy))
                act.activation(sq[:, 0:4, :], ry, ACT.Square).then_inc(sem("ret_sq"), 1)
                act.wait_ge(sem("ret_sum"), h + 1)
                rstd_from(rstd[:, :], colb[:, 2, 0:T], 1.0 / RET_V).then_inc(sem("ret_r_ready"), 1)

            def dil_tables(r):
                act.wait_ge(sem("dil_angles"), 1)
                act.activation(dcs, dang[:, 0:2, :], ACT.Sin).then_inc(sem("dil_sincos"), 1)

            def dil_rope(r):
                i = r["i"]
                act.wait_ge(sem("dil_turned"), i + 1)
                dst = (qt if i < 6 else kt_)[:, 2 * (i % 6):2 * (i % 6) + 2, :]
                act.activation(dst, aux[:, :].rearrange("p (a b) -> p a b", b=T), ACT.Copy).then_inc(sem("dil_turn_copied"), 1)

            def dil(r):
                for a in range(DIL_S):
                    act.wait_ge(sem("dil_max"), a + 1)
                    for j in range(NT):
                        at, n = (0, 3 * P) if j == 0 else (3 * P, 6 * P)
                        ins = act.activation(ds_[:, at:at + n], ds_[:, at:at + n], ACT.Exp,
                                             bias=dneg[:, 2 * a + j:2 * a + j + 1],
                                             accum_out=drow[:, 8 * j + a:8 * j + a + 1])
                    ins.then_inc(sem("dil_p"), 1)
                    act.wait_ge(sem("dil_p_turned"), a + 1)
                    if a:
                        act.wait_ge(sem("dil_pv"), a)
                    act.activation(dp, colb[:, :, :].rearrange("p a b -> p (a b)")[:, 0:9 * P], ACT.Copy)\
                        .then_inc(sem("dil_pt"), 1)

            run = {"panel": panel, "norm_sum": norm_sum, "fill": fill, "op_hi": op_hi_, "gates": gates, "rg": rg_,
                   "hg": hg, "gd": gd, "ret_tables": ret_tables, "ret_head": ret_head, "dil_tables": dil_tables,
                   "dil_rope": dil_rope, "dil": dil}
            act.wait_ge(sem("cols_loaded"), 16)
            act.wait_ge(sem("setup_a"), 1)
            act.activation(small[0:8, 34:36], c("a_log_rows", 0, 2, 8), ACT.Exp)
            act.activation(small[:, 36:40], small[:, 36:40], ACT.Exp, scale=-1.0)
            act.activation(small[:, 112:116], small[:, 112:116], ACT.Exp).then_inc(sem("setup_e"), 1)
            for what, r in schedule:
                if what in run:
                    run[what](r)

        @block.vector
        def _(dve):
            chain = [0]

            def link(ins):
                chain[0] += 1
                ins.then_inc(sem("dve_chain"), 1)
                dve.wait_ge(sem("dve_chain"), chain[0])

            normed = [0]
            tt, ts, stt = dve.tensor_tensor, dve.tensor_scalar, dve.scalar_tensor_tensor

            def split_lo(r):
                p = r["p"]
                dve.wait_ge(sem("w_hi_ready"), p + 1)
                tt(split_view(w_lo, r), raw[:, p % RAW_SLOTS, 0:r["kt"] * r["nc"]],
                   split_view(w_hi, r).bitcast(F32), ALU.subtract).then_inc(sem("w_lo_ready"), 1)

            def panel(r):
                if r["p"] == 0:
                    split_lo(r)
                if r["p"] + 1 < n_panels:
                    split_lo(panels[r["p"] + 1])
                if r["kind"] == "row" or r["by"] != "dve":
                    return
                dve.wait_ge(sem("panel_used"), r["p"] + 1)
                src = colb[:, r["c"] % 3, :]
                what = r["evac"]
                if what[0] == "h":
                    n = what[1]
                    dve.wait_ge(sem("act_evac"), what[2])
                    if n >= 2:
                        dve.wait_ge(sem("op_hi_ready"), n - 1)
                        dve.wait_ge(sem("op_ready"), n - 1)
                    tt(hid[:, n % 2, :], act_t[:, n % 2, :], src, ALU.mult).then_inc(sem("dve_evac"), 1)
                else:
                    dve.tensor_copy(what[1], src[0:what[3], 0:T]).then_inc(sem("dve_evac"), 1)
                    dve.wait_ge(sem("dve_evac"), r["n"])

            def relu2(r):
                dve.wait_ge(sem("act_evac"), r["evac"])
                n = r["r"]
                dve.wait_ge(sem("op_hi_ready"), n - 1)
                dve.wait_ge(sem("op_ready"), n - 1)
                tt(hid[:, n % 2, :], act_t[:, n % 2, :], act_t[:, n % 2, :], ALU.mult).then_inc(sem("hid_ready"), 1)

            def op_lo_(r):
                r = r["r"]
                dve.wait_ge(sem("op_hi_ready"), r["r"] + 1)
                src = r["src"]
                if isinstance(src, tuple):
                    src = u32[:, 2 * src[1]:2 * src[1] + 2, :].rearrange("p a b -> p (a b)")
                s = r["r"] % OP_SLOTS
                tt(op_lo[:, s, :], src, op_hi[:, s, :].bitcast(F32), ALU.subtract).then_inc(sem("op_ready"), 1)

            def fill(r):
                if r["src"] == "norm":
                    dve.wait_ge(sem("rstd_ready"), r["norm"])
                    for i in range(KD):
                        ins = stt(u32[:, i, :], x[:, i, :], c(r["gain"], r["at"] + i), rstd[:, :], ALU.mult, ALU.mult)
                        if i % 2:
                            ins.then_inc(sem("u32_ready"), 1)
                for i in range(4):
                    dve.wait_ge(sem("u_hi_ready"), 4 * (r["n"] - 1) + i + 1)
                    s = slice(2 * i, 2 * i + 2)
                    tt(u_lo[:, s, :], u32[:, s, :], u_hi[:, s, :].bitcast(F32), ALU.subtract).then_inc(sem("u_ready"), 1)

            def x_update(r):
                xf = x[:, :, :].rearrange("p a b -> p (a b)")
                if r["kind"] in ("half", "whole"):
                    dve.wait_ge(sem("panel_used"), r["panel"])
                    stt(xf, acc[:, :], 0.5 if r["kind"] == "half" else 1.0, xf, ALU.mult, ALU.add)\
                        .then_inc(sem("x_updated"), 1)
                    dve.wait_ge(sem("x_updated"), r["nx"])
                    return
                dve.wait_ge(sem("rstd_ready"), r["norm"])
                if r["kind"] == "final":
                    for i in range(KD):
                        ins = stt(x[:, i, :], x[:, i, :], c("norm_final", i), rstd[:, :], ALU.mult, ALU.mult)
                else:
                    for i in range(KD):
                        src = acc[:, T * i:T * i + T] if r["kind"] == "post" else gate_t[:, i, :]
                        ins = stt(u32[:, i, :], src, c(r["gain"], i), rstd[:, :], ALU.mult, ALU.mult)
                    if r["kind"] == "post":
                        normed[0] += 1
                        ins.then_inc(sem("acc_normed"), 1)
                        dve.wait_ge(sem("acc_normed"), normed[0])
                    else:
                        link(ins)
                    ins = tt(xf, xf, u32[:, :, :].rearrange("p a b -> p (a b)"), ALU.add)
                ins.then_inc(sem("x_updated"), 1)
                dve.wait_ge(sem("x_updated"), r["nx"])

            def log1p(o, e, s, q, t):
                link(ts(t, e, 2.0, None, ALU.add))
                link(dve.reciprocal(s, t))
                link(tt(s, s, e, ALU.mult))
                link(tt(q, s, s, ALU.mult))
                link(ts(o, q, 2.0 / 17, 2.0 / 15, ALU.mult, ALU.add))
                for d in (13, 11, 9, 7, 5, 3, 1):
                    link(tt(o, o, q, ALU.mult))
                    link(ts(o, o, 2.0 / d, None, ALU.add))
                link(tt(o, o, s, ALU.mult))

            def gates(r):
                l = r["l"]
                g = gt
                dve.memset(gd_in[:, :, 0:3], 0.0)
                dve.memset(rg_in[:, :, 0:3], 0.0)
                ts(g[2], g[0], c("dt_rows", l, 1, 8), None, ALU.add).then_inc(sem("gates_z"), 1)
                dve.wait_ge(sem("gates_e"), l + 1)
                log1p(g[5], g[4], g[6], g[7], g[8])
                link(stt(g[5], g[2], 0.0, g[5], ALU.max, ALU.add))
                link(ts(g[5], g[5], neg_a[:, l:l + 1], None, ALU.mult))
                for j in range(NT):
                    s = slice(P * j, P * j + P)
                    ins = dve.tensor_tensor_scan(g[6][:, s], k("ones", 0, P, 8), g[5][:, s], 0.0, ALU.mult, ALU.add)
                link(ins)
                link(ts(g[7], g[6], k("sel_g", 0, 1, 8), None, ALU.mult))
                stt(gates_c[:, :], g[1], k("sel_beta", 0, 1, 8), g[7], ALU.mult, ALU.add).then_inc(sem("gates_ready"), 1)

            def gates_read(l):
                dve.wait_ge(sem("gates_spread"), l + 1)
                link(dve.tensor_copy(gcol, aux[:, 0:16]))
                dve.tensor_copy(rbeta, acc[:, 0:1024].rearrange("p (h t) -> p h t", t=T))
                for j in range(NT):
                    for h in range(GD_H):
                        ins = stt(dt_[:, j, P * h:P * h + P], acc[:, 1024 + T * h + P * j:1024 + T * h + P * j + P],
                                  gcol[:, 8 * j + 4 + h:8 * j + 5 + h], k("neg", 0, P), ALU.subtract, ALU.add)
                ins.then_inc(sem("gates_diff"), 1)

            def conv(dst, src, w, b=None):
                if b is None:
                    link(ts(dst, src[:, 0:T], w(0), None, ALU.mult))
                else:
                    link(ts(dst, src[:, 0:T], w(0), b, ALU.mult, ALU.add))
                for i in range(1, 4):
                    ins = stt(dst, src[:, i:i + T], w(i), dst, ALU.mult, ALU.add)
                    if i < 3:
                        link(ins)
                return ins

            def rg_(r):
                l = r["l"]
                dve.wait_ge(sem("act_evac"), r["evac"])
                for t in range(2):
                    ins = conv(xc[:, t, :], rg_in[:, t, :], lambda i: c("rg_conv_w", 8 * l + 2 * i + t), c("rg_conv_b", 2 * l + t))
                ins.then_inc(sem("rg_xc"), 1)
                dve.wait_ge(sem("rg_gates_read"), l + 1)
                ts(rsq, rt, 1e-19, None, ALU.max).then_inc(sem("rg_tc"), 1)
                link(ts(rrcp, rt, 1.0, None, ALU.add))
                link(dve.reciprocal(rrcp, rrcp))
                link(ts(ra, rt, -1.0, 1.0, ALU.mult, ALU.add))
                link(tt(ra, ra, rrcp, ALU.mult))
                link(tt(rbx, r_ig[:, 2:4, :], xc, ALU.mult))
                link(tt(rbx, rbx, rrcp, ALU.mult))
                dve.wait_ge(sem("rg_root"), l + 1)
                link(stt(rbx, rsq, 2.0, rbx, ALU.mult, ALU.mult))
                for t in range(2):
                    ins = dve.tensor_tensor_scan(rh[:, t, :], ra[:, t, :], rbx[:, t, :], 0.0, ALU.mult, ALU.add)
                link(ins)
                link(tt(u32[:, 6:8, :], rh, rgate, ALU.mult))

            def hg(r):
                l = r["l"]
                for t in range(2):
                    ins = ts(hf[:, t, :], hf[:, t, :], omlb[:, 2 * l + t:2 * l + t + 1], lbv[:, 2 * l + t:2 * l + t + 1], ALU.mult, ALU.add)
                link(ins)
                ts(hcum, hf, 1e-19, None, ALU.max).then_inc(sem("hg_f"), 1)
                dve.tensor_scalar(hk, hf, -1.0, 1.0, ALU.mult, ALU.add)
                dve.memset(hat, 0.0)
                link(ts(hq, hq, HG_D ** -0.5, None, ALU.mult))
                dve.wait_ge(sem("hg_logf"), l + 1)
                for t in range(2):
                    ins = dve.tensor_tensor_scan(hf[:, t, :], k("ones").broadcast_to([P, T]), hcum[:, t, :], 0.0, ALU.mult, ALU.add)
                link(ins)
                cum = hf
                for i, n in enumerate([P] + LEVELS):
                    cv = cum.rearrange("p a b -> p (a b)").rearrange("p (b two n) -> p b two n", two=2, n=n)
                    dv = de[:, i, :].rearrange("p (b two n) -> p b two n", two=2, n=n)
                    mid = bc(cv[:, :, 0, n - 1], 2, n)
                    tt(dv[:, :, 1, :], cv[:, :, 1, :], mid, ALU.subtract)
                    ins = tt(dv[:, :, 0, :], mid, cv[:, :, 0, :], ALU.subtract)
                ins.then_inc(sem("hg_de"), 1)
                dve.wait_ge(sem("hg_e"), l + 1)

                def products(i):
                    n = ([P] + LEVELS)[i]
                    dv = de[:, i, :].rearrange("p (b two n) -> p b two n", two=2, n=n)
                    qv = hq.rearrange("p a b -> p (a b)").rearrange("p (b two n) -> p b two n", two=2, n=n)
                    kv = hk.rearrange("p a b -> p (a b)").rearrange("p (b two n) -> p b two n", two=2, n=n)
                    tt(dv[:, :, 1, :], dv[:, :, 1, :], qv[:, :, 1, :], ALU.mult)
                    tt(dv[:, :, 0, :], dv[:, :, 0, :], kv[:, :, 0, :], ALU.mult).then_inc(sem("hg_qk"), 1)

                products(0)
                for i in range(9):
                    if i < 7:
                        products(i + 1)
                    dve.wait_ge(sem("hg_scores"), 9 * l + i + 1)
                    for par in range(2):
                        b = bank[2 * (i % 2) + par]
                        if i == 0:
                            ins = dve.tensor_copy(hax[:, par, :], b[:, 0:2 * P])
                        else:
                            m = ident if i == 8 else k("masks", P * (i - 1), P)
                            ins = dve.copy_predicated(hat[:, par, :, :], bc(m.bitcast(I32), 1, 4),
                                                      b.rearrange("p (a b) -> p a b", b=P))
                    ins.then_inc(sem("hg_copied"), 1)
                    dve.wait_ge(sem("hg_copied"), 9 * l + i + 1)
                dve.wait_ge(sem("hg_rstd"), l + 1)
                for t in range(2):
                    ins = stt(u32[:, t, :], ho[:, t, :], c("hg_norm_w", l), act_t[:, 0, T * t:T * t + T], ALU.mult, ALU.mult)
                link(ins)
                link(tt(u32[:, 0:2, :], u32[:, 0:2, :], hgate, ALU.mult))

            def gd(r):
                l = r["l"]
                for i in range(12):
                    ins = conv(qkv[:, i, :], gd_in[:, i, :], lambda t: c("gd_conv_w", 48 * l + 12 * t + i))
                ins.then_inc(sem("gd_conv"), 1)
                gates_read(l)
                tt(qkv[:, 0:8, :], qkv[:, 0:8, :], sq[:, :, :], ALU.mult).then_inc(sem("gd_qk"), 1)
                dve.wait_ge(sem("gd_qk"), l + 1)
                dve.wait_ge(sem("gates_read"), l + 1)
                link(tt(eq, qkv[:, 0:4, P:T], eq, ALU.mult))
                dve.wait_ge(sem("gd_scores"), l + 1)
                for j in range(NT):
                    link(tt(lt[:, j, :], bank[j], dt_[:, j, :], ALU.mult))
                    rb = rbeta[:, :, P * j:P * j + P]
                    l4 = lt[:, j, :].rearrange("p (h t) -> p h t", t=P)
                    tt(sc[:, j, :], bank[2 + j], dt_[:, j, :], ALU.mult)
                    link(tt(l4, l4, rb, ALU.mult))
                    x4 = xt[:, j, :].rearrange("p (h t) -> p h t", t=P)
                    n4 = ntm[:, j, :].rearrange("p (h t) -> p h t", t=P)
                    link(tt(n4, l4, bc(k("masks", 6 * P, P), 1, 4), ALU.mult))
                    tt(x4, bc(ident, 1, 4), n4, ALU.subtract).then_inc(sem("gd_x"), 1)
                for i in range(1, 7):
                    for j in range(NT):
                        l4 = lt[:, j, :].rearrange("p (h t) -> p h t", t=P)
                        n4 = ntm[:, j, :].rearrange("p (h t) -> p h t", t=P)
                        m = bc(k("masks", (6 - i) * P, P), 1, 4)
                        if i == 1:
                            dve.wait_ge(sem("gd_x0"), 2 * l + j + 1)
                            tt(n4, l4, m, ALU.mult)
                            dve.tensor_copy(xi[:, j, :], bank[j]).then_inc(sem("gd_x"), 1)
                        else:
                            dve.wait_ge(sem("gd_z"), 12 * l + 2 * (i - 2) + j + 1)
                            tt(n4, l4, m, ALU.mult)
                            tt(xi[:, j, :], xi[:, j, :], bank[j], ALU.subtract)
                            tt(xt[:, j, :], xt[:, j, :], bank[2 + j], ALU.subtract).then_inc(sem("gd_x"), 1)
                for j in range(NT):
                    dve.wait_ge(sem("gd_z"), 12 * l + 10 + j + 1)
                    link(tt(xt[:, j, :], xt[:, j, :], bank[2 + j], ALU.subtract))
                dve.wait_ge(sem("gd_tok"), 3 * l + 3)
                v4 = [vtok[:, j, :].rearrange("p (h t) -> p h t", t=P) for j in range(2)]

                def col(v):
                    return bc(v, 2, P)

                def beta(j):
                    return col(gcol[:, 8 * j:8 * j + 4])

                tt(rr, v4[0], beta(0), ALU.mult).then_inc(sem("gd_r"), 1)
                dve.wait_ge(sem("gd_vn"), 2 * l + 1)
                dve.tensor_copy(vn[:, 0, :], bank[0])
                d4 = dt_[:, 0, :].rearrange("p (h t) -> p h t", t=P)
                tt(vs, bank[0].rearrange("p (h t) -> p h t", t=P), col(d4[:, :, P - 1]), ALU.mult).then_inc(sem("gd_vs"), 1)
                dve.wait_ge(sem("gd_ks"), l + 1)
                link(tt(tmp, bank[2].rearrange("p (h t) -> p h t", t=P), col(gexp), ALU.mult))
                link(tt(tmp, v4[1], tmp, ALU.subtract))
                tt(rr, tmp, beta(1), ALU.mult).then_inc(sem("gd_r"), 1)
                dve.wait_ge(sem("gd_vn"), 2 * l + 2)
                dve.tensor_copy(vn[:, 1, :], bank[3]).then_inc(sem("gd_vn_copied"), 1)
                dve.wait_ge(sem("gd_orstd"), l + 1)
                link(stt(u32[:, 2:6, :], go, c("gd_norm_w", l), grs, ALU.mult, ALU.mult))
                tt(u32[:, 2:6, :], u32[:, 2:6, :], z, ALU.mult).then_inc(sem("u32_ready"), 1)

            def reduced(o, tmp_, shift_turns, shift):
                magic = 12582912.0
                link(ts(o, tmp_, 1.0 / (2 * np.pi), shift_turns, ALU.mult, ALU.add))
                link(ts(o, o, magic, None, ALU.add))
                return ts(o, o, magic, None, ALU.subtract)

            def angles(ang, turns, o, shift_turns, shift):
                link(reduced(turns, ang, shift_turns, shift))
                c1, c2 = 6.28125, float(np.float32(2 * np.pi - 6.28125))
                c3 = float(2 * np.pi - 6.28125 - np.float64(np.float32(2 * np.pi - 6.28125)))
                link(stt(o, turns, -c1, ang, ALU.mult, ALU.add))
                link(stt(o, turns, -c2, o, ALU.mult, ALU.add))
                link(stt(o, turns, -c3, o, ALU.mult, ALU.add))
                link(ts(o, o, shift, 3.1415925, ALU.add, ALU.min))
                return ts(o, o, -3.1415925, None, ALU.max)

            def ret_tables(r):
                dve.wait_ge(sem("pos_loaded"), 16)
                dve.wait_ge(sem("posc_loaded"), 16)
                link(dve.tensor_copy(angt[:, 2, :], posf.bitcast(I32)))
                link(ts(angt[:, 2, :], angt[:, 2, :], k("inv_freq"), None, ALU.mult))
                link(angles(angt[:, 2, :], angt[:, 3, :], angt[:, 0, :], 0.0, 0.0))
                angles(angt[:, 2, :], angt[:, 3, :], angt[:, 1, :], 0.25, float(np.pi / 2)).then_inc(sem("ret_angles"), 1)

            def rope(r):
                dve.wait_ge(sem("ret_sincos"), 1)
                dve.wait_ge(sem("act_evac"), r["evac"])
                s4, c4 = bc(csin, 1, 4), bc(ccos, 1, 4)
                a, b = sq[:, 0:4, :], sq[:, 4:8, :]
                for i in range(2):
                    v = rqk[:, 8 * i:8 * i + 8, :].rearrange("p (h two) t -> p h two t", two=2)
                    x1, x2 = v[:, :, 0, :], v[:, :, 1, :]
                    tt(a, x1, s4, ALU.mult)
                    link(tt(b, x2, s4, ALU.mult))
                    tt(x1, x1, c4, ALU.mult)
                    link(tt(x2, x2, c4, ALU.mult))
                    tt(x1, x1, b, ALU.subtract)
                    tt(x2, x2, a, ALU.add).then_inc(sem("roped"), 1)
                    dve.wait_ge(sem("roped"), i + 1)

            def ret_head(r):
                h = r["h"]
                if h == 0:
                    dve.wait_ge(sem("dec_loaded"), 16)
                dve.wait_ge(sem("ret_scores"), h + 1)
                tt(rp[:, h % 2, :], aux[:, 0:3 * P], dec[:, h, :], ALU.mult).then_inc(sem("ret_p_ready"), 1)
                dve.wait_ge(sem("ret_r_ready"), h + 1)
                link(tt(ry, ry, bc(rstd[:, :], 1, 4), ALU.mult))
                tt(ry, ry, rg[:, 4 * h:4 * h + 4, :], ALU.mult).then_inc(sem("ret_y_ready"), 1)
                dve.wait_ge(sem("ret_y_ready"), h + 1)

            def ya_(r):
                dve.wait_ge(sem("panel_used"), r["panel"])
                dve.tensor_copy(ya.rearrange("p a b -> p (a b)"), acc[:, :]).then_inc(sem("ya_ready"), 1)
                dve.wait_ge(sem("ya_ready"), 1)

            def dil_tables(r):
                n = NT * DIL_HALF
                link(dve.tensor_copy(small[:, 42:44], posc.bitcast(I32)))
                for j in range(NT):
                    ins = ts(dang[:, 2, DIL_HALF * j:DIL_HALF * (j + 1)], k("freqs", 0, DIL_HALF), small[:, 42 + j:43 + j], None, ALU.mult)
                link(ins)
                link(angles(dang[:, 2, :], dang[:, 3, :], dang[:, 0, :], 0.0, 0.0))
                angles(dang[:, 2, :], dang[:, 3, :], dang[:, 1, :], 0.25, float(np.pi / 2)).then_inc(sem("dil_angles"), 1)

            def dil_rope(r):
                i = r["i"]
                dve.wait_ge(sem("dil_sincos"), 1)
                dve.wait_ge(sem("act_evac"), r["evac"])
                for j in range(NT):
                    v = dtok[:, i % 2, PC * j:PC * j + PC].rearrange("p (h d) -> p h d", d=DIL_D)
                    x1, x2 = v[:, :, 0:DIL_HALF], v[:, :, DIL_HALF:2 * DIL_HALF]
                    s = bc(dcs[:, 0, DIL_HALF * j:DIL_HALF * (j + 1)], 1, 4)
                    co = bc(dcs[:, 1, DIL_HALF * j:DIL_HALF * (j + 1)], 1, 4)
                    a = drop[:, 2 * j, 0:32].rearrange("p (h d) -> p h d", d=DIL_HALF)
                    b = drop[:, 2 * j + 1, 0:32].rearrange("p (h d) -> p h d", d=DIL_HALF)
                    tt(a, x1, s, ALU.mult)
                    link(tt(b, x2, s, ALU.mult))
                    tt(x1, x1, co, ALU.mult)
                    link(tt(x2, x2, co, ALU.mult))
                    tt(x1, x1, b, ALU.subtract)
                    ins = tt(x2, x2, a, ALU.add)
                ins.then_inc(sem("dil_roped"), 1)

            def dil(r):
                dve.wait_ge(sem("dmask_loaded"), 16)
                for a in range(DIL_S):
                    dve.wait_ge(sem("dil_scores"), a + 1)
                    if a:
                        dve.wait_ge(sem("dil_p_turned"), a)
                    stt(ds_[:, 0:3 * P], acc[:, 0:3 * P], DIL_D ** -0.5, dmask[:, 0:3 * P], ALU.mult, ALU.add)
                    stt(ds_[:, 3 * P:9 * P], acc[:, 512:512 + 6 * P], DIL_D ** -0.5, dmask[:, 3 * P:9 * P], ALU.mult, ALU.add)\
                        .then_inc(sem("dil_masked"), 1)
                    dve.wait_ge(sem("dil_masked"), a + 1)
                    dve.tensor_reduce(dmax[:, 2 * a:2 * a + 1], ds_[:, 0:3 * P], AX.X, ALU.max)
                    link(dve.tensor_reduce(dmax[:, 2 * a + 1:2 * a + 2], ds_[:, 3 * P:9 * P], AX.X, ALU.max))
                    ts(dneg[:, 2 * a:2 * a + 2], dmax[:, 2 * a:2 * a + 2], -1.0, None, ALU.mult).then_inc(sem("dil_max"), 1)
                dve.wait_ge(sem("dil_p"), DIL_S)
                link(dve.reciprocal(drinv, drow))
                dve.wait_ge(sem("dil_pv"), DIL_S)
                for j in range(NT):
                    o = (bank[3] if j == 0 else aux[:, :]).rearrange("p (a d) -> p a d", d=DIL_D)
                    ins = tt(do[:, j, :].rearrange("p (a d) -> p a d", d=DIL_D), o,
                             bc(drinv[:, 8 * j:8 * j + 8], 2, DIL_D), ALU.mult)
                ins.then_inc(sem("dil_o"), 1)
                dve.wait_ge(sem("dil_o_turned"), 1)
                for i in range(2):
                    dve.tensor_copy(u32[:, 2 * i:2 * i + 2, :].rearrange("p a b -> p (a b)"), bank[i]).then_inc(sem("dil_ot"), 1)
                dve.wait_ge(sem("dil_ot"), 2)

            def gate_ya(r):
                i = r["i"]
                dve.wait_ge(sem("act_evac"), r["evac"])
                s = ya[:, 2 * i:2 * i + 2, :].rearrange("p a b -> p (a b)")
                tt(s, s, act_t[:, i % 2, :], ALU.mult).then_inc(sem("ya_gated"), 1)

            def mixed(r):
                dve.wait_ge(sem("act_evac"), r["evac"])
                dve.wait_ge(sem("ya_gated"), 4)
                dve.wait_ge(sem("panel_used"), r["panel"])
                flat = sga.rearrange("p a b -> p (a b)")
                tt(flat, flat, acc[:, :], ALU.mult).then_inc(sem("acc_mixed"), 1)
                dve.wait_ge(sem("acc_mixed"), 1)
                tt(u32[:, :, :], sga, ya, ALU.add).then_inc(sem("u32_ready"), 1)

            def ple(r):
                dve.wait_ge(sem("act_evac"), r["evac"])
                dve.wait_ge(sem("panel_used"), r["panel"])
                g = gate_t.rearrange("p a b -> p (a b)")
                tt(g, g, acc[:, :], ALU.mult).then_inc(sem("gated_ready"), 1)

            run = {"panel": panel, "op_lo": op_lo_, "fill": fill, "x_update": x_update, "gates": gates, "rg": rg_,
                   "hg": hg, "gd": gd, "ret_tables": ret_tables, "rope": rope, "ret_head": ret_head, "ya": ya_,
                   "dil_tables": dil_tables, "dil_rope": dil_rope, "dil": dil, "gate_ya": gate_ya, "mixed": mixed,
                   "ple": ple, "relu2": relu2}

            dve.memset(bias_eps, EPS)
            dve.memset(bias_lndk, float(np.log(GD_D ** -0.5)))
            dve.wait_ge(sem("cols_loaded"), 16)
            dve.wait_ge(sem("cst_loaded"), 16)
            lam = c("rg_lambda", 0, 4)
            link(ts(small[:, 32 + 4:40], lam, -1.0, None, ALU.mult))
            link(tt(small[:, 36:40], small[:, 36:40], lam, ALU.max))
            lb = c("hg_lb", 0, 4)
            link(tt(small[:, 116:118], lb[:, 0:2], lb[:, 2:4], ALU.max))
            tt(small[:, 112:114], lb[:, 0:2], small[:, 116:118], ALU.subtract)
            tt(small[:, 114:116], lb[:, 2:4], small[:, 116:118], ALU.subtract).then_inc(sem("setup_a"), 1)
            dve.wait_ge(sem("setup_e"), 1)
            ts(neg_a, small[0:8, 34:36], -1.0, None, ALU.mult)
            log1p(small[:, 120:124], small[:, 36:40], small[:, 124:128], small[:, 128:132], small[:, 132:136])
            link(ts(small[:, 124:128], lam, -1.0, 0.0, ALU.mult, ALU.max))
            link(tt(sp4, small[:, 120:124], small[:, 124:128], ALU.add))
            link(ts(sp4, sp4, 4.0, None, ALU.mult))
            e0, e1 = small[:, 112:114], small[:, 114:116]
            link(tt(small[:, 116:118], e0, e1, ALU.add))
            link(dve.reciprocal(small[:, 118:120], small[:, 116:118]))
            tt(e0, e0, small[:, 118:120], ALU.mult)
            link(tt(e1, e1, small[:, 118:120], ALU.mult))
            dve.memset(lbv[:, 0:2], 0.0)
            link(tt(e1, e0, e1, ALU.add))
            link(tt(lbv[:, 2:4], e1, e0, ALU.subtract))
            link(ts(omlb, lbv, -1.0, 1.0, ALU.mult, ALU.add))
            for what, r in schedule:
                if what in run:
                    run[what](r)


def kernel(**inputs):
    import concourse.bacc as bacc
    from concourse.bass_utils import run_bass_kernel_spmd as run

    i = {n: np.asarray(a) for n, a in inputs.items()}
    f = np.float32

    def columns(a, n):
        return np.ascontiguousarray(a.reshape(-1, P).T)

    def rows(a):
        o = np.zeros((P, DEPTH), f)
        o[GD_H:2 * GD_H] = a.T
        return o

    tab = {n: columns(i[n], 0) for n, _ in COLS if n in i and n not in ("hg_norm_w",)}
    tab["hg_norm_w"] = np.ascontiguousarray(np.concatenate([i["hg_norm_w"]] * 2, 1).T)
    tab["dt_rows"], tab["a_log_rows"] = rows(i["gd_dt_bias"]), rows(i["gd_a_log"])
    rg_w = np.zeros((P, DEPTH, 2, 2, P), f)
    for g, name in enumerate(("rg_wr", "rg_wi")):
        for n in range(4):
            s = slice(64 * (n % 2), 64 * (n % 2) + 64)
            for l in range(DEPTH):
                rg_w[s, l, g, n // 2, s] = i[name][l, n]
    cst, decay, dil_mask = shape_constants()
    data = {
        "x_t": i["x"][0].T.reshape(KD, P, T).transpose(1, 0, 2),
        "p_t": i["p_2"][0, 0].T.reshape(2, P, T).transpose(1, 0, 2),
        "columns": np.concatenate([tab[n] for n, _ in COLS], 1), "constants": cst, "decay": decay,
        "dil_mask": dil_mask, "rg_w": rg_w.reshape(P, -1), "positions": i["positions_2"],
        "positions_c": i["positions_2"].reshape(NT, P).T,
    }
    for n in ("ffn1_gate", "ffn1_up", "ffn1_down", "w_in", "w_out", "ffn2_gate", "ffn2_up", "ffn2_down", "w_in_2",
              "w_ret_out_2", "w_dil_out_2", "w_o_2", "w_up_2", "w_down_2", "w_ple_gate_2", "w_ple_in_2"):
        data[n] = i[n]
    nc = bacc.Bacc("TRN2", target_bir_lowering=False, num_devices=1)
    data = {n: np.ascontiguousarray(a) for n, a in data.items()}
    ap = {n: nc.dram_tensor(n, a.shape, mybir.dt.from_np(a.dtype), kind="ExternalInput").ap() for n, a in data.items()}
    out = nc.dram_tensor("out", (P, KD, T), F32, kind="ExternalOutput").ap()
    build(nc, ap, out)
    r = run(nc, [data], core_ids=[0])
    y = r.results[0]["out"]
    return np.ascontiguousarray(y.transpose(2, 1, 0).reshape(1, T, D))
```

```python
from contextlib import ExitStack

import numpy as np

import concourse.bass as bass
from concourse import mybir

ALU = mybir.AluOpType
ACT = mybir.ActivationFunctionType
AX = mybir.AxisListType
F32 = mybir.dt.float32
F32R = mybir.dt.float32r
I32 = mybir.dt.int32

P = 128
T = 256
NT = T // P
D = 1024
KD = D // P
DEPTH = 2
D_FF = 2816
PC = 256
PANEL = KD * PC
EPS = 1e-6
LEVELS = [64, 32, 16, 8, 4, 2, 1]
HG_H, HG_D = 4, 64
GD_H, GD_D = 4, 128
GATES0 = 4 * 256 + 4 * 512
RGX0 = GATES0 + 2 * GD_H
RET_H, RET_QK, RET_V = 4, 256, 512
DIL_G, DIL_S, DIL_D = 3, 8, 64
DIL_HALF = DIL_D // 4 // 2
RAW_SLOTS, SPLIT_SLOTS, OP_SLOTS = 3, 2, 4

COLS = [("norm_ffn1", 16), ("norm_mix", 16), ("norm_ffn2", 16), ("norm_final", 8), ("g_pre_mix_2", 8),
        ("g_post_mix_2", 8), ("g_pre_mlp_2", 8), ("g_post_mlp_2", 8), ("g_pre_ple_2", 8),
        ("g_post_ple_2", 8), ("b_gate_2", 16), ("b_ple_gate_2", 8), ("hg_lb", 4), ("hg_norm_w", 2),
        ("gd_norm_w", 2), ("gd_conv_w", 96), ("rg_conv_w", 16), ("rg_conv_b", 4), ("rg_br", 4),
        ("rg_bi", 4), ("rg_lambda", 4), ("dt_rows", 2), ("a_log_rows", 2)]
COL_AT = {}
NCOL = 0
for _name, _n in COLS:
    COL_AT[_name] = NCOL
    NCOL += _n

CONSTS = [("ident", P), ("ones", P), ("head_ones", P), ("masks", len(LEVELS) * P), ("neg", P),
          ("sel", 8 * P), ("sel_beta", 1), ("sel_g", 1), ("inv_freq", 1), ("freqs", DIL_HALF)]
CONST_AT = {}
NCONST = 0
for _name, _n in CONSTS:
    CONST_AT[_name] = NCONST
    NCONST += _n
N_DECAY = RET_H * 3 * P
N_DIL = DIL_G * 3 * P


def shape_constants():
    f = np.float32
    c = np.zeros((P, NCONST), f)

    def put(name, a):
        c[:, CONST_AT[name]:CONST_AT[name] + a.shape[1]] = a

    s, t = np.arange(P)[:, None], np.arange(P)[None, :]
    put("ident", (s == t).astype(f))
    put("ones", np.ones((P, P), f))
    put("head_ones", (s // HG_D == t // HG_D).astype(f))
    put("masks", np.concatenate([((s // (2 * n) == t // (2 * n)) & (s // n < t // n)).astype(f) for n in LEVELS], 1))
    put("neg", np.where(s <= t, 0, -1e30).astype(f))
    sel = np.zeros((P, 8, P), f)
    for i in range(8):
        sel[i, i] = 1
    put("sel", sel.reshape(P, -1))
    rows = np.arange(P)[:, None]
    put("sel_beta", (rows < GD_H).astype(f))
    put("sel_g", ((rows >= GD_H) & (rows < 2 * GD_H)).astype(f))
    put("inv_freq", (f(1) / f(10000) ** np.linspace(0, 1, P, dtype=f))[:, None].astype(f))
    put("freqs", np.broadcast_to(f(500000) ** (-np.arange(0, 2 * DIL_HALF, 2, dtype=f) / f(2 * DIL_HALF)), (P, DIL_HALF)))
    decay = np.zeros((P, RET_H, 3, P), np.float64)
    for h in range(RET_H):
        g = np.log1p(-(2.0 ** (-5.0 - h)))
        for b, shift in enumerate((0, P, 0)):
            dist = t - s + shift
            decay[:, h, b] = np.where(dist >= 0, np.exp(np.maximum(dist, 0) * g), 0) * RET_QK ** -0.5
    q = np.arange(P)[:, None]
    parts = []
    for j in range(2):
        for window, dil in ((128, 1), (512, 4), (2048, 16)):
            dist = q + j * P - np.arange((j + 1) * P)[None, :]
            ok = (dist >= 0) & (dist % dil == 0) & (dist // dil <= window // dil)
            parts.append(np.where(ok, 0, -1e30))
    return c, decay.reshape(P, -1).astype(f), np.concatenate(parts, 1).astype(f)


def build(nc, ap, out, stop_at=None):
    ctx = ExitStack()
    with ctx:
        def sb(name, shape, dt=F32):
            return ctx.enter_context(nc.sbuf_tensor(name, shape, dt))

        sems = {}

        def sem(name):
            if name not in sems:
                sems[name] = ctx.enter_context(nc.semaphore(name))
            return sems[name]

        raw = sb("raw", [P, RAW_SLOTS, PANEL])
        w_hi = sb("w_hi", [P, SPLIT_SLOTS, PANEL], F32R)
        w_lo = sb("w_lo", [P, SPLIT_SLOTS, PANEL], F32R)
        u_hi = sb("u_hi", [P, KD, T], F32R)
        u_lo = sb("u_lo", [P, KD, T], F32R)
        op_hi = sb("op_hi", [P, OP_SLOTS, 2 * T], F32R)
        op_lo = sb("op_lo", [P, OP_SLOTS, 2 * T], F32R)
        x = sb("x", [P, KD, T])
        u32 = sb("u32", [P, KD, T])
        sq = sb("sq", [P, KD, T])
        act_t = sb("act_t", [P, 2, 2 * T])
        hid = sb("hid", [P, 2, 2 * T])
        rstd = sb("rstd", [P, T])
        lnv = sb("lnv", [P, T])
        cols = sb("cols", [P, NCOL])
        cst = sb("cst", [P, NCONST])
        rg_w = sb("rg_w_sb", [P, DEPTH * 4 * P])
        gates_c = sb("gates_c", [8, T])
        small = sb("small", [P, 160])
        bias = sb("bias", [P, 3])
        arena = sb("arena", [P, 17450])
        acc = ctx.enter_context(nc.psum_tensor("acc", [P, KD * T], F32))
        colb = ctx.enter_context(nc.psum_tensor("colb", [P, 3, 2 * T], F32))
        aux = ctx.enter_context(nc.psum_tensor("aux", [P, 2 * T], F32))
        bank = [acc[:, 512 * i:512 * i + 512] for i in range(4)]

        def c(name, i=0, n=1, rows=P):
            o = COL_AT[name] + i
            return cols[0:rows, o:o + n]

        def k(name, i=0, n=1, rows=P):
            o = CONST_AT[name] + i
            return cst[0:rows, o:o + n]

        ident, ones, head_ones = k("ident", 0, P), k("ones", 0, P), k("head_ones", 0, P)
        bias_eps, bias_lndk, bias_hpi = bias[:, 0:1], bias[:, 1:2], bias[:, 2:3]

        def view(at, *shape):
            n = int(np.prod(shape))
            v = arena[:, at:at + n]
            if len(shape) == 2:
                v = v.rearrange("p (a b) -> p a b", b=shape[1])
            if len(shape) == 3:
                v = v.rearrange("p (a b c) -> p a b c", b=shape[1], c=shape[2])
            return v

        def bc(v, axis, n):
            s = list(v.shape)
            s.insert(axis, n)
            return v.unsqueeze(axis).broadcast_to(s)

        z = hid[:, :, :].rearrange("p a (b t) -> p (a b) t", t=T)
        qkv = view(0, 12, T)
        A0 = 12 * T
        gd_in = view(A0, 12, T + 3)
        lt, sc, xi = view(A0, 2, 4 * P), view(A0 + 1024, 2, 4 * P), view(A0 + 2048, 2, 4 * P)
        vtok, ktok, go = lt, view(A0 + 2048, 4, P), view(A0 + 2048, 4, T)
        A1 = A0 + 12 * (T + 3)
        eq, xt, ntm = view(A1, 4, P), view(A1 + 512, 2, 4 * P), view(A1 + 1536, 2, 4 * P)
        yl, rbeta = view(A1 + 2560, 2, 4 * P), view(A1 + 2560, 4, T)
        dt_, vn = view(A1 + 3584, 2, 4 * P), view(A1 + 3584, 2, 4 * P)
        rr, vs = view(A1 + 1536, 4, P), view(A1 + 2048, 4, P)
        st, tmp = view(A1 + 2560, 4, P), view(A1 + 3072, 4, P)
        grs = lt.rearrange("p a (b t) -> p (a b) t", t=T)
        A2 = A1 + 4608
        hf, hq, hgate = view(A2, 2, T), view(A2 + 512, 2, T), view(A2 + 1024, 2, T)
        hv, rgate = view(A2 + 1536, NT, T), view(A2 + 2048, 2, T)
        rg_in = view(A2 + 2560, 2, T + 3)
        A3 = A2 + 2560 + 2 * (T + 3)
        hk, hcum, ho = view(A3, 2, T), view(A3 + 512, 2, T), view(A3 + 512, 2, T)
        hat = view(A3 + 1024, 2, 4, P)
        hax = view(A3 + 2048, 2, 2 * P)
        xc, r_ig = view(A3, 2, T), view(A3 + 512, 4, T)
        rt, rrcp, rsq = view(A3 + 1536, 2, T), view(A3 + 2048, 2, T), view(A3 + 2560, 2, T)
        gt = [act_t[0:8, 0, 0:T], act_t[0:8, 0, T:2 * T], act_t[0:8, 1, 0:T], act_t[0:8, 1, T:2 * T]] + \
            [arena[0:8, A1 + T * i:A1 + T * i + T] for i in range(5)]
        de = sq[:, :, :].rearrange("p (s a) t -> p s (a t)", s=4)
        hg_scores = [colb[:, 0, :], colb[:, 1, :], colb[:, 2, :], aux[:, :]]
        hrs = act_t[:, 0, :]
        gcol = small[:, 0:16]
        gexp = small[:, 16:20]
        dlast = small[:, 136:140]
        sp4 = small[:, 20:24]
        lbv, omlb = small[:, 24:28], small[:, 28:32]
        neg_a = small[0:8, 32:34]

        rqk = view(0, 16, T)
        rv = view(4096, NT, RET_H * RET_V)
        rg = view(8192, 16, T)
        rp = view(12288, 2, 3 * P)
        ry = [u32[:, 0:4, :], u32[:, 4:8, :]]
        dec = view(14080, RET_H, 3 * P)
        csin, ccos = view(15616, 2, T)[:, 0, :], view(15616, 2, T)[:, 1, :]
        posf = view(16128, 1, T)[:, 0, :]
        angt = view(16384, 4, T)
        qt, kt_ = view(0, 12, T), view(3072, 12, T)
        av = view(6144, NT, DIL_G * DIL_S * DIL_D)
        dtok = view(9216, 2, 2 * T)
        ds_ = [view(10240, 1, 9 * P)[:, 0, :], sq[:, :, :].rearrange("p a b -> p (a b)")[:, 0:9 * P]]
        dp = view(11392, 1, 9 * P)[:, 0, :]
        do = view(12544, NT, DIL_S * DIL_D)
        ya = view(13568, KD, T)
        dmask = view(15616, 1, N_DIL)[:, 0, :]
        dcs = view(16768, 2, NT * DIL_HALF)
        dang = view(16800, 4, NT * DIL_HALF)
        drop = view(16864, 4, NT * 4 * DIL_HALF)[:, :, 0:NT * 4 * DIL_HALF]
        sga = view(0, KD, T)
        gate_t = view(2048, KD, T)
        p32 = view(6144, 2, T)
        posc = small[:, 40:42]
        dmax = small[:, 48:64]
        drow = small[:, 64:80]
        drinv = small[:, 80:96]
        dneg = small[:, 96:112]

        schedule, panels, ops = [], [], []
        n_col = n_act = n_dve = n_row = 0
        count = {"norm": 0, "fill": 0, "x": 0, "u32": 0, "normed": 0, "group": 0}
        acc_reader = [None]

        def panel(src, kt, ncols, kind, xop, ready, **more):
            nonlocal n_col, n_act, n_dve, n_row
            r = dict(p=len(panels), src=src, kt=kt, nc=ncols, kind=kind, xop=xop, ready=ready, **more)
            if kind != "row":
                r["c"] = n_col
                n_col += 1
                if r["by"] == "act":
                    n_act += 1
                    r["n"] = n_act
                else:
                    n_dve += 1
                    r["n"] = n_dve
            else:
                n_row += 1
            panels.append(r)
            schedule.append(("panel", r))
            return r

        def step(name, **more):
            schedule.append((name, dict(panel=len(panels), nx=count["x"], op=len(ops), **more)))

        def u_op(kk):
            return u_hi[:, kk, :], u_lo[:, kk, :]

        def fill(src_kind, **more):
            count["fill"] += 1
            step("fill", n=count["fill"], src=src_kind, u32=count["u32"], **more)
            count["u32"] += 4 if src_kind == "norm" else 1
            return count["fill"]

        def norm_sum(src):
            count["norm"] += 1
            step("norm_sum", n=count["norm"], src=src, x=count["x"], group=count["group"])
            return count["norm"]

        def pre_norm(gain, at):
            n = norm_sum("x")
            return fill("norm", gain=gain, at=at, norm=n)

        def x_update(kind, **more):
            count["x"] += 1
            step("x_update", kind=kind, group=count["group"], **more)
            if kind in ("half", "whole"):
                acc_reader[0] = ("x_updated", 4 * count["x"])
            if kind == "post":
                count["normed"] += 1
                acc_reader[0] = ("acc_normed", count["normed"])

        def operand(src, ready):
            r = dict(r=len(ops), src=src, ready=ready)
            ops.append(r)
            return r

        def op_tiles(r):
            def get(kk):
                s = r["r"] % OP_SLOTS
                return op_hi[:, s, T * kk:T * kk + T], op_lo[:, s, T * kk:T * kk + T]
            return get

        def kpn(w):
            return w.rearrange("(k p) n -> p k n", p=P)

        def row_gemm_panel(w, i, r, first, last, base=None):
            if r is not None:
                ready = [("op_ready", r["r"] + 1)]
                r["panel"] = len(panels)
                get = op_tiles(r)
            else:
                ready = base[0]
                get = (lambda kk, i=i: base[1](2 * i + kk))
            if first and acc_reader[0]:
                ready = ready + [acc_reader[0]]
            panel(kpn(w)[:, 2 * i:2 * i + 2, :], 2, D, "row", get, ready, first=first, last=last)
            if last:
                count["group"] += 1

        def ffn(layer, gain, gate, up, down):
            f = pre_norm(gain, KD * layer)
            n = D_FF // PC
            todo = None
            for i in range(n):
                g = panel(kpn(gate)[:, :, i * PC:(i + 1) * PC], KD, PC, "A", u_op, [("u_ready", 4 * f)],
                          by="act", evac=("silu_h", len(ops)))
                if i:
                    step("op_lo", r=todo)
                u = panel(kpn(up)[:, :, i * PC:(i + 1) * PC], KD, PC, "A", u_op, [], by="dve",
                          evac=("h", len(ops), g["n"]))
                r = operand(hid[:, len(ops) % 2, :], [("dve_evac", u["n"])])
                if i:
                    row_gemm_panel(down, i - 1, todo, i == 1, False)
                step("op_hi", r=r)
                todo = r
            step("op_lo", r=todo)
            row_gemm_panel(down, n - 1, todo, n == 1, True)
            x_update("half")

        def mixer(l):
            f = pre_norm("norm_mix", KD * l)
            w = kpn(ap["w_in"][l])
            ready = [("u_ready", 4 * f)]

            def cp(c0, n, kind, evac, by="act"):
                return panel(w[:, :, c0:c0 + n], KD, n, kind, u_op, ready, by=by, evac=evac)["n"]

            def gd_panel(i):
                return cp(1024 + i * PC, PC, "A", ("copy", gd_in[:, 2 * i:2 * i + 2, 3:], 0))

            cp(GATES0, P, "A", ("copy", gt[0], 0, 8), by="dve")
            b = cp(RGX0, PC, "A", ("copy", rg_in[:, :, 3:], 0))
            e = gd_panel(0)
            step("gate_rows", l=l)
            for i in range(1, 6):
                n = gd_panel(i)
                step("gd_conv", l=l, i=i - 1, evac=e)
                e = n
                if i == 2:
                    step("rg_conv", l=l, evac=b)
            d = cp(RGX0 + PC, PC, "A", ("gelu", rgate))
            step("gd_conv", l=l, i=5, evac=e)
            step("gd_ss", l=l)
            cp(256, PC, "A", ("sigmoid", hf))
            step("rg_gates", l=l)
            e = cp(0, PC, "A", ("silu", hq))
            step("spread", l=l)
            step("rg_scan", l=l, evac=d)
            for i in range(2):
                cp(2560 + i * PC, PC, "A", ("silu", z[:, 2 * i:2 * i + 2, :]))
                if i == 0:
                    step("gd_scores", l=l)
            cp(768, PC, "A", ("silu", hgate))
            step("gd_x0", l=l)
            step("hg_prep", l=l, evac=e)
            e = cp(512, PC, "B", ("copy", hv, 0))
            for n in range(3):
                step("hg_exponents", l=l, n=n)
            n = 0
            for i in range(1, 7):
                step("gd_y", l=l, i=i)
                for half in range(2):
                    if n < 9 and (half == 0 or i <= 3):
                        step("hg_level", l=l, n=n, evac=e)
                        if n + 3 < 8:
                            step("hg_exponents", l=l, n=n + 3)
                        n += 1
                    if half == 0:
                        step("gd_z", l=l, i=i)
            step("hg_out", l=l)
            step("gd_chunks", l=l)
            f = fill("y")
            for i in range(4):
                row_gemm_panel(ap["w_out"][l], i, None, i == 0, i == 3, ([("u_ready", 4 * f)], u_op))
            x_update("whole")

        for l in range(DEPTH):
            ffn(l, "norm_ffn1", ap["ffn1_gate"][l], ap["ffn1_up"][l], ap["ffn1_down"][l])
            if stop_at == "ffn1":
                break
            mixer(l)
            if stop_at == "mix":
                break
            ffn(l, "norm_ffn2", ap["ffn2_gate"][l], ap["ffn2_up"][l], ap["ffn2_down"][l])
            if stop_at == "layer":
                break

        def second_block():
            n = norm_sum("x")
            x_update("final", norm=n)
            if stop_at == "first":
                return
            f = pre_norm("g_pre_mix_2", 0)
            w = kpn(ap["w_in_2"][0])
            ready = [("u_ready", 4 * f)]

            def cp(c0, kind, evac):
                return panel(w[:, :, c0:c0 + PC], KD, PC, kind, u_op, ready, by="act", evac=evac)["n"]

            step("ret_tables")
            for i in range(8):
                e = cp(i * PC, "A", ("copy", rqk[:, 2 * i:2 * i + 2, :], 0))
            step("rope", evac=e)
            for i in range(8):
                e = cp(2048 + i * PC, "B", ("copy", rv[:, :, i * PC:(i + 1) * PC], 0))
            for i in range(8):
                e = cp(4096 + i * PC, "A", ("silu", rg[:, 2 * i:2 * i + 2, :]))
            rs = {}

            def ret_rows(h, i):
                row_gemm_panel(ap["w_ret_out_2"][0], 2 * h + i, rs[h][i], h + i == 0, (h, i) == (RET_H - 1, 1))

            step("ret_scores", h=0, evac=e)
            step("ret_values", h=0)
            for h in range(RET_H):
                if h + 1 < RET_H:
                    step("ret_scores", h=h + 1, evac=e)
                step("ret_norm", h=h)
                if h:
                    ret_rows(h - 1, 1)
                if h + 1 < RET_H:
                    step("ret_values", h=h + 1)
                rs[h] = []
                for i in range(2):
                    r = operand(ry[h % 2][:, 2 * i:2 * i + 2, :].rearrange("p a b -> p (a b)"), [("ret_y_ready", h + 1)])
                    step("op_hi", r=r)
                    step("op_lo", r=r)
                    rs[h].append(r)
                ret_rows(h, 0)
            ret_rows(RET_H - 1, 1)
            step("ya")
            acc_reader[0] = ("ya_ready", 1)
            step("dil_tables")
            base = 6144
            for i in range(12):
                e = cp(base + i * PC, "B", ("copy", dtok[:, i % 2, :].rearrange("p (a b) -> p a b", b=PC), 1))
                step("dil_rope", i=i, evac=e)
                if i:
                    step("dil_turn", i=i - 1)
            for i in range(6):
                e = cp(base + 3072 + i * PC, "B", ("copy", av[:, :, i * PC:(i + 1) * PC], 0))
                if i == 0:
                    step("dil_turn", i=11)
            step("dil", evac=e)
            for i in range(4):
                r = panel(w[:, :, 10752 + i * PC:10752 + (i + 1) * PC], KD, PC, "A", u_op, [], by="act",
                          evac=("gate_bias", act_t[:, i % 2, :], "b_gate_2", 2 * i, i))
                step("gate_ya", i=i, evac=r["n"])
            for i in range(4):
                e = cp(11776 + i * PC, "A", ("gate_bias", sga[:, 2 * i:2 * i + 2, :], "b_gate_2", KD + 2 * i, None))
            for i in range(2):
                r = operand(("dil_o", i), [("dil_ot", i + 1)])
                step("op_hi", r=r)
                step("op_lo", r=r)
                row_gemm_panel(ap["w_dil_out_2"][0], i, r, i == 0, i == 1)
            step("mixed", evac=e)
            acc_reader[0] = ("acc_mixed", 1)
            f = fill("y")
            for i in range(4):
                row_gemm_panel(ap["w_o_2"][0], i, None, i == 0, i == 3, ([("u_ready", 4 * f)], u_op))
            n = norm_sum("acc")
            x_update("post", norm=n, gain="g_post_mix_2")
            if stop_at == "mix2":
                return
            f = pre_norm("g_pre_mlp_2", 0)
            todo = None
            for i in range(16):
                panel(kpn(ap["w_up_2"][0])[:, :, i * PC:(i + 1) * PC], KD, PC, "A", u_op,
                      [("u_ready", 4 * f)], by="act", evac=("relu", len(ops)))
                step("relu2", r=len(ops), evac=n_act)
                if i:
                    row_gemm_panel(ap["w_down_2"][0], i - 1, todo, i == 1, False)
                r = operand(hid[:, len(ops) % 2, :], [("hid_ready", i + 1)])
                todo = r
                step("op_hi", r=r)
                step("op_lo", r=r)
            row_gemm_panel(ap["w_down_2"][0], 15, todo, False, True)
            n = norm_sum("acc")
            x_update("post", norm=n, gain="g_post_mlp_2")
            if stop_at == "mlp2":
                return
            f = pre_norm("g_pre_ple_2", 0)
            step("load_p")
            r = operand(p32.rearrange("p a b -> p (a b)"), [("p_loaded", 16)])
            step("op_hi", r=r)
            step("op_lo", r=r)
            for i in range(4):
                e = panel(kpn(ap["w_ple_gate_2"][0])[:, :, i * PC:(i + 1) * PC], KD, PC, "A", u_op,
                          [("u_ready", 4 * f)], by="act",
                          evac=("gate_bias", gate_t[:, 2 * i:2 * i + 2, :], "b_ple_gate_2", 2 * i, None))["n"]
            row_gemm_panel(ap["w_ple_in_2"][0], 0, r, True, True)
            step("ple", evac=e)
            n = norm_sum("gated")
            x_update("post_gated", norm=n, gain="g_post_ple_2")

        if stop_at in (None, "first", "mix2", "mlp2"):
            second_block()
        n_x, n_panels = count["x"], len(panels)
        by_column = [r for r in panels if r["kind"] != "row"]

        def split_view(t, r):
            return t[:, r["p"] % SPLIT_SLOTS, 0:r["kt"] * r["nc"]]

        def col_bank_free(eng, n):
            r = by_column[n]
            eng.wait_ge(sem(f"{r['by']}_evac"), r["n"])

        def bank_done(eng, r, b):
            if b < 3:
                eng.wait_ge(sem("acc_bank"), 3 * (r["group"] - 1) + b + 1)
            else:
                eng.wait_ge(sem("panel_used"), r["panel"])

        block = ctx.enter_context(nc.Block())

        @block.sync
        def _(sp):
            sp.dma_start(x[:, :, :], ap["x_t"]).then_inc(sem("x_loaded"), 16)
            sp.dma_start(cols[:, :], ap["columns"]).then_inc(sem("cols_loaded"), 16)
            sp.dma_start(cst[:, :], ap["constants"]).then_inc(sem("cst_loaded"), 16)
            sp.dma_start(rg_w[:, :], ap["rg_w"]).then_inc(sem("rg_w_loaded"), 16)
            for what, r in schedule:
                if what == "panel":
                    p = r["p"]
                    if p >= RAW_SLOTS:
                        sp.wait_ge(sem("w_hi_ready"), p - RAW_SLOTS + 1)
                        sp.wait_ge(sem("w_lo_ready"), p - RAW_SLOTS + 1)
                    dst = raw[:, p % RAW_SLOTS, 0:r["kt"] * r["nc"]].rearrange("p (k n) -> p k n", k=r["kt"])
                    sp.dma_start(dst, r["src"]).then_inc(sem(f"raw_loaded{p % RAW_SLOTS}"), 16)
            sp.wait_ge(sem("x_updated"), 4 * n_x)
            sp.dma_start(out, x[:, :, :]).then_inc(sem("stored"), 16)
            sp.wait_ge(sem("stored"), 16)

        @block.gpsimd
        def _(pool):
            for what, r in schedule:
                if what == "ret_tables":
                    pool.wait_ge(sem("x_updated"), 4 * 7)
                    pool.dma_start(dec.rearrange("p a b -> p (a b)"), ap["decay"]).then_inc(sem("dec_loaded"), 16)
                    pool.dma_start(posf.bitcast(I32), ap["positions"].partition_broadcast(P)).then_inc(sem("pos_loaded"), 16)
                    pool.dma_start(posc.bitcast(I32), ap["positions_c"]).then_inc(sem("posc_loaded"), 16)
                if what == "dil_tables":
                    pool.wait_ge(sem("ya_ready"), 1)
                    pool.dma_start(dmask, ap["dil_mask"]).then_inc(sem("dmask_loaded"), 16)
                if what == "load_p":
                    pool.wait_ge(sem("x_updated"), 4 * 9)
                    pool.dma_start(p32, ap["p_t"]).then_inc(sem("p_loaded"), 16)

        @block.tensor
        def _(pe):
            def mm(o, a, b, start=True, stop=True):
                return pe.matmul(o, a, b, start=start, stop=stop, skip_group_check=True)

            def gemm(r):
                p = r["p"]
                for name, v in r["ready"]:
                    pe.wait_ge(sem(name), v)
                if r["kind"] != "row" and r["c"] >= 3:
                    col_bank_free(pe, r["c"] - 3)
                pe.wait_ge(sem("w_hi_ready"), p + 1)
                pe.wait_ge(sem("w_lo_ready"), p + 1)
                wh = split_view(w_hi, r).rearrange("p (k n) -> p k n", k=r["kt"])
                wl = split_view(w_lo, r).rearrange("p (k n) -> p k n", k=r["kt"])
                if r["kind"] == "row":
                    order = [(kk, m) for kk in range(r["kt"]) for m in range(KD)]
                    if r["last"]:
                        order = [(kk, m) for b in range(4) for kk in range(r["kt"]) for m in (2 * b, 2 * b + 1)]
                    for kk, m in order:
                        xh, xl = r["xop"](kk)
                        o = acc[:, T * m:T * m + T]
                        m_ = slice(P * m, P * m + P)
                        mm(o, wh[:, kk, m_], xh, r["first"] and kk == 0 and m % 2 == 0, False)
                        mm(o, wh[:, kk, m_], xl, False, False)
                        last = mm(o, wl[:, kk, m_], xh, False, r["last"] and kk == r["kt"] - 1)
                        if r["last"] and kk == r["kt"] - 1 and m % 2 and m < KD - 1:
                            last.then_inc(sem("acc_bank"), 1)
                else:
                    for m in range(max(r["nc"] // P, 1)):
                        o = colb[:, r["c"] % 3, T * m:T * m + T]
                        for kk in range(r["kt"]):
                            xh, xl = r["xop"](kk)
                            m_ = slice(P * m, P * m + P)
                            if r["kind"] == "A":
                                trio = ((wh[:, kk, m_], xh), (wh[:, kk, m_], xl), (wl[:, kk, m_], xh))
                            else:
                                trio = ((xh[:, m_], wh[:, kk, :]), (xl[:, m_], wh[:, kk, :]), (xh[:, m_], wl[:, kk, :]))
                            for i, (a, b) in enumerate(trio):
                                last = mm(o, a, b, kk == 0 and i == 0, kk == r["kt"] - 1 and i == 2)
                last.then_inc(sem("panel_used"), 1)

            def norm_sum(r):
                for kk in range(KD):
                    if kk % 2 == 0:
                        pe.wait_ge(sem("sq_ready"), 4 * (r["n"] - 1) + kk // 2 + 1)
                    last = mm(aux[:, 0:T], ones, sq[:, kk, :], kk == 0, kk == KD - 1)
                last.then_inc(sem("norm_summed"), 1)

            def gd_ss(r):
                l = r["l"]
                pe.wait_ge(sem("gd_sq"), 4 * l + 4)
                for i in range(8):
                    last = mm(acc[:, T * i:T * i + T], ones, sq[:, i, :])
                last.then_inc(sem("gd_ss"), 1)

            def rg_gates(r):
                l = r["l"]
                pe.wait_ge(sem("gd_rn"), l + 1)
                pe.wait_ge(sem("rg_xc"), l + 1)
                for g in range(2):
                    for t in range(2):
                        w = rg_w[:, (l * 4 + g * 2 + t) * P:(l * 4 + g * 2 + t + 1) * P]
                        last = mm(bank[g][:, T * t:T * t + T], w, xc[:, t, :])
                last.then_inc(sem("rg_gates"), 1)

            def spread(r):
                l = r["l"]
                pe.wait_ge(sem("gates_ready"), l + 1)
                pe.wait_ge(sem("rg_gates_read"), l + 1)
                for i in range(8):
                    mm(acc[:, T * i:T * i + T], k("sel", P * i, P, 8), gates_c[:, :])
                for j in range(NT):
                    last = pe.transpose(aux[:, 8 * j:8 * j + 8], gates_c[:, P * j:P * j + P], k("ident", 0, 8, 8))
                last.then_inc(sem("gates_spread"), 1)

            def gd_scores(r):
                l = r["l"]
                pe.wait_ge(sem("gates_read"), l + 1)
                pe.wait_ge(sem("gd_qk"), l + 1)
                for j in range(NT):
                    for h in range(GD_H):
                        kj = qkv[:, 4 + h, P * j:P * j + P]
                        mm(bank[j][:, P * h:P * h + P], kj, kj)
                        last = mm(bank[2 + j][:, P * h:P * h + P], kj, qkv[:, h, P * j:P * j + P])
                last.then_inc(sem("gd_scores"), 1)

            def gd_x0(r):
                l = r["l"]
                for j in range(NT):
                    pe.wait_ge(sem("gd_x"), 14 * l + j + 1)
                    for h in range(GD_H):
                        last = pe.transpose(bank[j][:, P * h:P * h + P], xt[:, j, P * h:P * h + P], ident)
                    last.then_inc(sem("gd_x0"), 1)

            def gd_y(r):
                l, i = r["l"], r["i"]
                for j in range(NT):
                    pe.wait_ge(sem("gd_x"), 14 * l + 2 * i + j + 1)
                    for h in range(GD_H):
                        s = slice(P * h, P * h + P)
                        last = mm(bank[j][:, s], ntm[:, j, s], xi[:, j, s])
                    last.then_inc(sem("gd_y"), 1)

            def gd_z(r):
                l, i = r["l"], r["i"]
                for j in range(NT):
                    pe.wait_ge(sem("gd_y_copied"), 12 * l + 2 * (i - 1) + j + 1)
                    for h in range(GD_H):
                        s = slice(P * h, P * h + P)
                        if i < 6:
                            mm(bank[j][:, s], xt[:, j, s], yl[:, j, s])
                        last = mm(bank[2 + j][:, s], yl[:, j, s], xt[:, j, s])
                    last.then_inc(sem("gd_z"), 1)

            def hg_level(r):
                l, n = r["l"], r["n"]
                if n == 0:
                    pe.wait_ge(sem("act_evac"), r["evac"])
                if n < 8:
                    pe.wait_ge(sem("hg_qk"), 8 * l + n + 1)
                if n >= 2:
                    pe.wait_ge(sem("hg_copied"), 9 * l + n - 1)
                for par in range(2):
                    rows = slice(64 * par, 64 * par + 64)
                    b = hg_scores[2 * (n % 2) + par]
                    for ch in range(2):
                        if n == 0:
                            e = de[rows, 0, T * ch:T * ch + T]
                            last = mm(b[:, P * ch:P * ch + P], e[:, 0:P], e[:, P:T])
                            continue
                        for j in range(NT):
                            if n < 8:
                                a = q = de[rows, n % 4, T * ch + P * j:T * ch + P * j + P]
                            else:
                                a, q = hk[rows, ch, P * j:P * j + P], hq[rows, ch, P * j:P * j + P]
                            last = mm(b[:, (2 * ch + j) * P:(2 * ch + j + 1) * P], a, q)
                last.then_inc(sem("hg_scores"), 1)

            def hg_out(r):
                l = r["l"]
                pe.wait_ge(sem("hg_copied"), 9 * l + 9)
                for par in range(2):
                    for ch in range(2):
                        h = 2 * ch + par
                        o = colb[64 * par:64 * par + 64, 0, T * ch:T * ch + T]
                        mm(o[:, 0:P], hv[:, 0, 64 * h:64 * h + 64], hat[:, par, 2 * ch, :])
                        mm(o[:, P:T], hv[:, 0, 64 * h:64 * h + 64], hax[:, par, P * ch:P * ch + P], True, False)
                        last = mm(o[:, P:T], hv[:, 1, 64 * h:64 * h + 64], hat[:, par, 2 * ch + 1, :], False, True)
                last.then_inc(sem("hg_o"), 1)
                for n in range(3):
                    if n:
                        pe.wait_ge(sem("gd_tok"), 3 * l + n)
                    else:
                        pe.wait_ge(sem("gd_vfree"), l + 1)
                    for h in range(GD_H):
                        src = qkv[:, 8 + h, P * n:P * n + P] if n < 2 else qkv[:, 4 + h, 0:P]
                        last = pe.transpose(aux[:, P * h:P * h + P], src, ident)
                    last.then_inc(sem("gd_turned"), 1)

            def gd_chunks(r):
                l = r["l"]
                hs = [slice(P * h, P * h + P) for h in range(GD_H)]

                def new_values(j, b):
                    pe.wait_ge(sem("gd_r"), 2 * l + j + 1)
                    for h in range(GD_H):
                        last = mm(bank[b][:, hs[h]], xt[:, j, hs[h]], rr[:, h, :])
                    last.then_inc(sem("gd_vn"), 1)

                new_values(0, 0)
                pe.wait_ge(sem("hg_sq"), l + 1)
                mm(colb[:, 1, :], head_ones, sq[:, 0:2, :].rearrange("p a b -> p (a b)")).then_inc(sem("hg_sum"), 1)
                pe.wait_ge(sem("gd_vs"), l + 1)
                for h in range(GD_H):
                    last = mm(bank[1][:, hs[h]], ktok[:, h, :], vs[:, h, :])
                last.then_inc(sem("gd_state"), 1)
                pe.wait_ge(sem("gd_state_copied"), l + 1)
                for h in range(GD_H):
                    last = mm(bank[2][:, hs[h]], qkv[:, 4 + h, P:T], st[:, h, :])
                last.then_inc(sem("gd_ks"), 1)
                new_values(1, 3)
                pe.wait_ge(sem("gd_vn_copied"), l + 1)
                for h in range(GD_H):
                    o = bank[h // 2][:, T * (h % 2):T * (h % 2) + T]
                    mm(o[:, 0:P], vn[:, 0, hs[h]], sc[:, 0, hs[h]])
                    mm(o[:, P:T], vn[:, 1, hs[h]], sc[:, 1, hs[h]], True, False)
                    last = mm(o[:, P:T], st[:, h, :], eq[:, h, :], False, True)
                last.then_inc(sem("gd_o"), 1)
                pe.wait_ge(sem("gd_osq"), l + 1)
                for h in range(GD_H):
                    last = mm(acc[:, 1024 + T * h:1024 + T * h + T], ones, sq[:, 4 + h, :])
                last.then_inc(sem("gd_osum"), 1)

            def ret_scores(r):
                h = r["h"]
                if h == 0:
                    pe.wait_ge(sem("roped"), 2)
                    pe.wait_ge(sem("act_evac"), r["evac"])
                for s0, n, at in ((0, T, 0), (P, P, T)):
                    for i in range(2):
                        last = mm(aux[:, at:at + n], rqk[:, 8 + 2 * h + i, s0:s0 + P], rqk[:, 2 * h + i, s0:T], i == 0, i == 1)
                last.then_inc(sem("ret_scores"), 1)

            def ret_values(r):
                h = r["h"]
                pe.wait_ge(sem("ret_p_ready"), h + 1)
                if h:
                    pe.wait_ge(sem("ret_sq"), h)
                pr = rp[:, h % 2, :]
                for i in range(4):
                    o = colb[:, i // 2, T * (i % 2):T * (i % 2) + T]
                    e = slice(RET_V * h + P * i, RET_V * h + P * i + P)
                    mm(o, rv[:, 0, e], pr[:, 0:T], True, False)
                    last = mm(o[:, P:T], rv[:, 1, e], pr[:, T:T + P], False, True)
                last.then_inc(sem("ret_y"), 1)

            def ret_norm(r):
                h = r["h"]
                pe.wait_ge(sem("ret_sq"), h + 1)
                if h:
                    pe.wait_ge(sem("ret_r_ready"), h)
                for i in range(4):
                    last = mm(colb[:, 2, 0:T], ones, sq[:, i, :], i == 0, i == 3)
                last.then_inc(sem("ret_sum"), 1)

            def dil_turn(r):
                i = r["i"]
                pe.wait_ge(sem("dil_roped"), i + 1)
                if i:
                    pe.wait_ge(sem("dil_turn_copied"), i)
                d = dtok[:, i % 2, :]
                for j in range(NT):
                    for t in range(2):
                        last = pe.transpose(aux[:, T * t + P * j:T * t + P * j + P], d[:, PC * j + P * t:PC * j + P * t + P], ident)
                last.then_inc(sem("dil_turned"), 1)

            def dil(r):
                pe.wait_ge(sem("dil_turn_copied"), 12)
                pe.wait_ge(sem("act_evac"), r["evac"])
                pe.wait_ge(sem("ya_ready"), 1)

                def scores(a):
                    rows = slice(64 * (a % 2), 64 * (a % 2) + 64)
                    if a:
                        pe.wait_ge(sem("dil_masked"), a)
                    for j in range(NT):
                        for g in range(DIL_G):
                            t = 4 * g + a // 2
                            n = P * (j + 1)
                            o = acc[:, 512 * j + n * g:512 * j + n * g + n]
                            last = mm(o, qt[rows, t, P * j:P * j + P], kt_[rows, t, 0:n])
                    last.then_inc(sem("dil_scores"), 1)

                def turn(a):
                    pe.wait_ge(sem("dil_p"), a + 1)
                    if a:
                        pe.wait_ge(sem("dil_pt"), a)
                    for g in range(DIL_G):
                        for b, at in enumerate((P * g, 3 * P + T * g, 3 * P + T * g + P)):
                            i = 3 * g + b
                            last = pe.transpose(colb[:, i // 4, P * (i % 4):P * (i % 4) + P], ds_[a % 2][:, at:at + P], ident)
                    last.then_inc(sem("dil_p_turned"), 1)

                def values(a):
                    pe.wait_ge(sem("dil_pt"), a + 1)
                    for j in range(NT):
                        o = (bank[3] if j == 0 else aux)[:, 64 * a:64 * a + 64]
                        for g in range(DIL_G):
                            v = slice(64 * (8 * g + a), 64 * (8 * g + a) + 64)
                            for s in range(j + 1):
                                last = mm(o, dp[:, P * (3 * g + j + s):P * (3 * g + j + s + 1)], av[:, s, v],
                                          g == 0 and s == 0, g == DIL_G - 1 and s == j)
                    last.then_inc(sem("dil_pv"), 1)

                scores(0)
                scores(1)
                for a in range(DIL_S):
                    turn(a)
                    if a + 2 < DIL_S:
                        scores(a + 2)
                    values(a)
                pe.wait_ge(sem("dil_o"), 1)
                for t in range(4):
                    for j in range(NT):
                        last = pe.transpose(acc[:, T * t + P * j:T * t + P * j + P], do[:, j, P * t:P * t + P], ident)
                last.then_inc(sem("dil_o_turned"), 1)

            run = {"panel": gemm, "norm_sum": norm_sum, "gd_ss": gd_ss, "rg_gates": rg_gates,
                   "spread": spread, "gd_scores": gd_scores, "gd_x0": gd_x0, "gd_y": gd_y, "gd_z": gd_z,
                   "hg_level": hg_level, "hg_out": hg_out, "gd_chunks": gd_chunks, "ret_scores": ret_scores,
                   "ret_values": ret_values, "ret_norm": ret_norm, "dil_turn": dil_turn, "dil": dil}
            pe.wait_ge(sem("cst_loaded"), 16)
            pe.wait_ge(sem("rg_w_loaded"), 16)
            for what, r in schedule:
                if what in run:
                    run[what](r)

        @block.scalar
        def _(act):
            chain = [0]

            def link(ins):
                chain[0] += 1
                ins.then_inc(sem("act_chain"), 1)
                act.wait_ge(sem("act_chain"), chain[0])

            def split_hi(r):
                p = r["p"]
                act.wait_ge(sem(f"raw_loaded{p % RAW_SLOTS}"), 16 * (p // RAW_SLOTS + 1))
                if p >= SPLIT_SLOTS:
                    act.wait_ge(sem("panel_used"), p - SPLIT_SLOTS + 1)
                act.activation(split_view(w_hi, r), raw[:, p % RAW_SLOTS, 0:r["kt"] * r["nc"]], ACT.Copy)\
                    .then_inc(sem("w_hi_ready"), 1)

            def act_t_free(n):
                if n >= 2:
                    name, v = ops[n - 2]["ready"][0]
                    act.wait_ge(sem(name), v)

            def panel(r):
                if r["p"] == 0:
                    split_hi(r)
                if r["p"] + 1 < n_panels:
                    split_hi(panels[r["p"] + 1])
                if r["kind"] == "row" or r["by"] != "act":
                    return
                act.wait_ge(sem("panel_used"), r["p"] + 1)
                src = colb[:, r["c"] % 3, :]
                src2 = src.rearrange("p (a b) -> p a b", b=T)
                what = r["evac"]
                if what[0] == "silu_h":
                    act_t_free(what[1])
                    ins = act.activation(act_t[:, what[1] % 2, :], src, ACT.Silu)
                elif what[0] == "relu":
                    act_t_free(what[1])
                    ins = act.activation(act_t[:, what[1] % 2, :], src, ACT.Relu)
                elif what[0] == "gate_bias":
                    if what[4] is not None and what[4] >= 2:
                        act.wait_ge(sem("ya_gated"), what[4] - 1)
                    for m in range(2):
                        dst = what[1] if len(what[1].shape) == 3 else what[1].rearrange("p (a b) -> p a b", b=T)
                        ins = act.activation(dst[:, m, :], src2[:, m, :], ACT.Sigmoid, bias=c(what[2], what[3] + m))
                else:
                    fn = {"copy": ACT.Copy, "gelu": ACT.Gelu_apprx_tanh, "sigmoid": ACT.Sigmoid, "silu": ACT.Silu}[what[0]]
                    if what[0] == "copy" and what[2]:
                        i = r["c"] - first_dil
                        if i >= 2:
                            act.wait_ge(sem("dil_turned"), i - 1)
                    ins = act.activation(what[1], src2, fn)
                ins.then_inc(sem("act_evac"), 1)

            first_dil = next((r["c"] for r in by_column if r["evac"][0] == "copy" and r["evac"][2] == 1), 0)

            def rstd_from(o, s, scale, b2=0.0):
                link(act.activation(o, s, ACT.Ln, bias=bias_eps, scale=scale))
                return act.activation(o, o, ACT.Exp, scale=-0.5, bias=b2)

            def norm_sum(r):
                for b in range(4):
                    s = slice(2 * b, 2 * b + 2)
                    if r["src"] == "x":
                        if r["x"] == 0 and b == 0:
                            act.wait_ge(sem("x_loaded"), 16)
                        if r["x"]:
                            act.wait_ge(sem("x_updated"), 4 * (r["x"] - 1) + b + 1)
                        src = x[:, s, :]
                    elif r["src"] == "acc":
                        bank_done(act, r, b)
                        src = bank[b].rearrange("p (a t) -> p a t", t=T)
                    else:
                        act.wait_ge(sem("gated_ready"), b + 1)
                        src = gate_t[:, s, :]
                    act.activation(sq[:, s, :], src, ACT.Square).then_inc(sem("sq_ready"), 1)
                act.wait_ge(sem("norm_summed"), r["n"])
                rstd_from(rstd[:, :], aux[:, 0:T], 1.0 / D).then_inc(sem("rstd_ready"), 1)

            def fill(r):
                act.wait_ge(sem("panel_used"), r["panel"])
                for i in range(4):
                    act.wait_ge(sem("u32_ready"), r["u32"] + (i + 1 if r["src"] == "norm" else 1))
                    act.activation(u_hi[:, 2 * i:2 * i + 2, :], u32[:, 2 * i:2 * i + 2, :], ACT.Copy)\
                        .then_inc(sem("u_hi_ready"), 1)

            def op_hi_(r):
                r = r["r"]
                for name, v in r["ready"]:
                    act.wait_ge(sem(name), v)
                if r["r"] >= OP_SLOTS:
                    act.wait_ge(sem("panel_used"), ops[r["r"] - OP_SLOTS]["panel"] + 1)
                src = r["src"]
                if isinstance(src, tuple):
                    src = u32[:, 2 * src[1]:2 * src[1] + 2, :].rearrange("p a b -> p (a b)")
                act.activation(op_hi[:, r["r"] % OP_SLOTS, :], src, ACT.Copy).then_inc(sem("op_hi_ready"), 1)

            def gate_rows(r):
                l = r["l"]
                act.wait_ge(sem("gates_z"), l + 1)
                act.activation(gt[1], gt[0], ACT.Sigmoid).then_inc(sem("gates_sig"), 1)
                link(act.activation(gt[3], gt[2], ACT.Abs))
                act.activation(gt[4], gt[3], ACT.Exp, scale=-1.0).then_inc(sem("gates_e"), 1)

            def gd_conv(r):
                l, i = r["l"], r["i"]
                act.wait_ge(sem("gd_conv"), 6 * l + i + 1)
                s = slice(2 * i, 2 * i + 2)
                act.activation(qkv[:, s, :], qkv[:, s, :], ACT.Silu).then_inc(sem("gd_silu"), 1)
                if i < 4:
                    act.wait_ge(sem("gd_silu"), 6 * l + i + 1)
                    act.activation(sq[:, s, :], qkv[:, s, :], ACT.Square).then_inc(sem("gd_sq"), 1)

            def gd_ss(r):
                l = r["l"]
                act.wait_ge(sem("gd_ss"), l + 1)
                flat = sq[:, :, :].rearrange("p a b -> p (a b)")
                link(act.activation(flat, acc[:, :], ACT.Ln, bias=bias_eps))
                act.activation(flat[:, 0:1024], flat[:, 0:1024], ACT.Exp, scale=-0.5, bias=bias_lndk)
                act.activation(flat[:, 1024:2048], flat[:, 1024:2048], ACT.Exp, scale=-0.5).then_inc(sem("gd_rn"), 1)

            def rg_gates(r):
                l = r["l"]
                act.wait_ge(sem("rg_gates"), l + 1)
                for g in range(2):
                    for t in range(2):
                        ins = act.activation(r_ig[:, 2 * g + t, :], bank[g][:, T * t:T * t + T], ACT.Sigmoid,
                                             bias=c(("rg_br", "rg_bi")[g], 2 * l + t))
                ins.then_inc(sem("rg_gates_read"), 1)
                act.wait_ge(sem("rg_gates_read"), l + 1)
                for t in range(2):
                    ins = act.activation(rt[:, t, :], r_ig[:, t, :], ACT.Tanh, scale=sp4[:, 2 * l + t:2 * l + t + 1])
                ins.then_inc(sem("rg_tanh"), 1)

            def rg_scan(r):
                l = r["l"]
                act.wait_ge(sem("rg_tc"), l + 1)
                link(act.activation(rsq, rsq, ACT.Ln))
                act.activation(rsq, rsq, ACT.Exp, scale=0.5).then_inc(sem("rg_root"), 1)

            def spread(r):
                l = r["l"]
                act.wait_ge(sem("gates_diff"), l + 1)
                act.activation(dt_, dt_, ACT.Exp)
                act.activation(eq, acc[:, 1024:2048].rearrange("p (h t) -> p h t", t=T)[:, :, P:T], ACT.Exp)
                act.activation(gexp, gcol[:, 12:16], ACT.Exp).then_inc(sem("gates_read"), 1)

            def hg_prep(r):
                l = r["l"]
                act.wait_ge(sem("hg_f"), l + 1)
                act.activation(hcum, hcum, ACT.Ln).then_inc(sem("hg_logf"), 1)

            def hg_exponents(r):
                l, n = r["l"], r["n"]
                act.wait_ge(sem("hg_de"), 8 * l + n + 1)
                act.activation(de[:, n % 4, :], de[:, n % 4, :], ACT.Exp).then_inc(sem("hg_e"), 1)

            def gd_y(r):
                l, i = r["l"], r["i"]
                for j in range(NT):
                    act.wait_ge(sem("gd_y"), 12 * l + 2 * (i - 1) + j + 1)
                    act.activation(yl[:, j, :], bank[j], ACT.Copy).then_inc(sem("gd_y_copied"), 1)

            def hg_out(r):
                l = r["l"]
                act.wait_ge(sem("hg_o"), l + 1)
                link(act.activation(ho, colb[:, 0, :].rearrange("p (a b) -> p a b", b=T), ACT.Copy))
                act.activation(sq[:, 0:2, :], ho, ACT.Square).then_inc(sem("hg_sq"), 1)
                for n in range(3):
                    act.wait_ge(sem("gd_turned"), 3 * l + n + 1)
                    dst = vtok[:, n, :] if n < 2 else ktok.rearrange("p a b -> p (a b)")
                    act.activation(dst, aux[:, :], ACT.Copy).then_inc(sem("gd_tok"), 1)

            def gd_chunks(r):
                l = r["l"]
                act.wait_ge(sem("hg_sum"), l + 1)
                rstd_from(hrs, colb[:, 1, :], 1.0 / HG_D).then_inc(sem("hg_rstd"), 1)
                act.wait_ge(sem("gd_state"), l + 1)
                act.activation(st.rearrange("p a b -> p (a b)"), bank[1], ACT.Copy).then_inc(sem("gd_state_copied"), 1)
                act.wait_ge(sem("gd_o"), l + 1)
                link(act.activation(go.rearrange("p a b -> p (a b)"), acc[:, 0:1024], ACT.Copy))
                act.activation(sq[:, 4:8, :], go, ACT.Square).then_inc(sem("gd_osq"), 1)
                act.wait_ge(sem("gd_osum"), l + 1)
                rstd_from(grs.rearrange("p a b -> p (a b)"), acc[:, 1024:2048], 1.0 / GD_D).then_inc(sem("gd_orstd"), 1)

            def ret_tables(r):
                act.wait_ge(sem("ret_angles"), 1)
                act.activation(csin, angt[:, 0, :], ACT.Sin)
                act.activation(ccos, angt[:, 1, :], ACT.Sin).then_inc(sem("ret_sincos"), 1)

            def ret_values(r):
                h = r["h"]
                act.wait_ge(sem("ret_y"), h + 1)
                if h >= 2:
                    act.wait_ge(sem("op_ready"), r["op"] - 2)
                link(act.activation(ry[h % 2].rearrange("p a b -> p (a b)"), colb[:, 0:2, :].rearrange("p a b -> p (a b)"), ACT.Copy))
                act.activation(sq[:, 0:4, :], ry[h % 2], ACT.Square).then_inc(sem("ret_sq"), 1)

            def ret_norm(r):
                h = r["h"]
                act.wait_ge(sem("ret_sum"), h + 1)
                if h:
                    act.wait_ge(sem("ret_y_ready"), h)
                rstd_from(rstd[:, :], colb[:, 2, 0:T], 1.0 / RET_V).then_inc(sem("ret_r_ready"), 1)

            def dil_tables(r):
                act.wait_ge(sem("dil_angles"), 1)
                act.activation(dcs, dang[:, 0:2, :], ACT.Sin).then_inc(sem("dil_sincos"), 1)

            def dil_turn(r):
                i = r["i"]
                act.wait_ge(sem("dil_turned"), i + 1)
                dst = (qt if i < 6 else kt_)[:, 2 * (i % 6):2 * (i % 6) + 2, :]
                act.activation(dst, aux[:, :].rearrange("p (a b) -> p a b", b=T), ACT.Copy).then_inc(sem("dil_turn_copied"), 1)

            def dil(r):
                for a in range(DIL_S):
                    act.wait_ge(sem("dil_max"), a + 1)
                    d = ds_[a % 2]
                    for j in range(NT):
                        at, n = (0, 3 * P) if j == 0 else (3 * P, 6 * P)
                        ins = act.activation(d[:, at:at + n], d[:, at:at + n], ACT.Exp,
                                             bias=dneg[:, 2 * a + j:2 * a + j + 1],
                                             accum_out=drow[:, 8 * j + a:8 * j + a + 1])
                    ins.then_inc(sem("dil_p"), 1)
                    act.wait_ge(sem("dil_p_turned"), a + 1)
                    if a:
                        act.wait_ge(sem("dil_pv"), a)
                    act.activation(dp, colb[:, :, :].rearrange("p a b -> p (a b)")[:, 0:9 * P], ACT.Copy)\
                        .then_inc(sem("dil_pt"), 1)

            run = {"panel": panel, "norm_sum": norm_sum, "fill": fill, "op_hi": op_hi_, "gate_rows": gate_rows,
                   "gd_conv": gd_conv, "gd_ss": gd_ss, "rg_gates": rg_gates, "rg_scan": rg_scan, "spread": spread,
                   "hg_prep": hg_prep, "hg_exponents": hg_exponents, "gd_y": gd_y, "hg_out": hg_out,
                   "gd_chunks": gd_chunks, "ret_tables": ret_tables, "ret_values": ret_values,
                   "ret_norm": ret_norm, "dil_tables": dil_tables, "dil_turn": dil_turn, "dil": dil}
            act.wait_ge(sem("cols_loaded"), 16)
            act.wait_ge(sem("setup_a"), 1)
            act.activation(small[0:8, 34:36], c("a_log_rows", 0, 2, 8), ACT.Exp)
            act.activation(small[:, 36:40], small[:, 36:40], ACT.Exp, scale=-1.0)
            act.activation(small[:, 112:116], small[:, 112:116], ACT.Exp).then_inc(sem("setup_e"), 1)
            for what, r in schedule:
                if what in run:
                    run[what](r)

        @block.vector
        def _(dve):
            chain = [0]

            def link(ins):
                chain[0] += 1
                ins.then_inc(sem("dve_chain"), 1)
                dve.wait_ge(sem("dve_chain"), chain[0])

            normed = [0]
            tt, ts, stt = dve.tensor_tensor, dve.tensor_scalar, dve.scalar_tensor_tensor

            def split_lo(r):
                p = r["p"]
                dve.wait_ge(sem("w_hi_ready"), p + 1)
                tt(split_view(w_lo, r), raw[:, p % RAW_SLOTS, 0:r["kt"] * r["nc"]],
                   split_view(w_hi, r).bitcast(F32), ALU.subtract).then_inc(sem("w_lo_ready"), 1)

            def panel(r):
                if r["p"] == 0:
                    split_lo(r)
                if r["p"] + 1 < n_panels:
                    split_lo(panels[r["p"] + 1])
                if r["kind"] == "row" or r["by"] != "dve":
                    return
                dve.wait_ge(sem("panel_used"), r["p"] + 1)
                src = colb[:, r["c"] % 3, :]
                what = r["evac"]
                if what[0] == "h":
                    n = what[1]
                    dve.wait_ge(sem("act_evac"), what[2])
                    if n >= 2:
                        dve.wait_ge(sem("op_hi_ready"), n - 1)
                        dve.wait_ge(sem("op_ready"), n - 1)
                    tt(hid[:, n % 2, :], act_t[:, n % 2, :], src, ALU.mult).then_inc(sem("dve_evac"), 1)
                else:
                    dve.tensor_copy(what[1], src[0:what[3], 0:T]).then_inc(sem("dve_evac"), 1)
                    dve.wait_ge(sem("dve_evac"), r["n"])

            def relu2(r):
                dve.wait_ge(sem("act_evac"), r["evac"])
                n = r["r"]
                dve.wait_ge(sem("op_hi_ready"), n - 1)
                dve.wait_ge(sem("op_ready"), n - 1)
                tt(hid[:, n % 2, :], act_t[:, n % 2, :], act_t[:, n % 2, :], ALU.mult).then_inc(sem("hid_ready"), 1)

            def op_lo_(r):
                r = r["r"]
                dve.wait_ge(sem("op_hi_ready"), r["r"] + 1)
                src = r["src"]
                if isinstance(src, tuple):
                    src = u32[:, 2 * src[1]:2 * src[1] + 2, :].rearrange("p a b -> p (a b)")
                s = r["r"] % OP_SLOTS
                tt(op_lo[:, s, :], src, op_hi[:, s, :].bitcast(F32), ALU.subtract).then_inc(sem("op_ready"), 1)

            def fill(r):
                if r["src"] == "norm":
                    dve.wait_ge(sem("rstd_ready"), r["norm"])
                    for i in range(KD):
                        ins = stt(u32[:, i, :], x[:, i, :], c(r["gain"], r["at"] + i), rstd[:, :], ALU.mult, ALU.mult)
                        if i % 2:
                            ins.then_inc(sem("u32_ready"), 1)
                for i in range(4):
                    dve.wait_ge(sem("u_hi_ready"), 4 * (r["n"] - 1) + i + 1)
                    s = slice(2 * i, 2 * i + 2)
                    tt(u_lo[:, s, :], u32[:, s, :], u_hi[:, s, :].bitcast(F32), ALU.subtract).then_inc(sem("u_ready"), 1)

            def x_update(r):
                xf = x[:, :, :].rearrange("p a b -> p (a b)")
                if r["kind"] in ("half", "whole"):
                    for b in range(4):
                        bank_done(dve, r, b)
                        s = xf[:, 512 * b:512 * b + 512]
                        stt(s, bank[b], 0.5 if r["kind"] == "half" else 1.0, s, ALU.mult, ALU.add)\
                            .then_inc(sem("x_updated"), 1)
                    dve.wait_ge(sem("x_updated"), 4 * r["nx"])
                    return
                dve.wait_ge(sem("rstd_ready"), r["norm"])
                for i in range(KD):
                    if r["kind"] == "final":
                        ins = stt(x[:, i, :], x[:, i, :], c("norm_final", i), rstd[:, :], ALU.mult, ALU.mult)
                        if i % 2:
                            ins.then_inc(sem("x_updated"), 1)
                    else:
                        src = acc[:, T * i:T * i + T] if r["kind"] == "post" else gate_t[:, i, :]
                        ins = stt(u32[:, i, :], src, c(r["gain"], i), rstd[:, :], ALU.mult, ALU.mult)
                if r["kind"] != "final":
                    if r["kind"] == "post":
                        normed[0] += 1
                        ins.then_inc(sem("acc_normed"), 1)
                        dve.wait_ge(sem("acc_normed"), normed[0])
                    else:
                        link(ins)
                    for b in range(4):
                        s = slice(2 * b, 2 * b + 2)
                        tt(x[:, s, :], x[:, s, :], u32[:, s, :], ALU.add).then_inc(sem("x_updated"), 1)
                dve.wait_ge(sem("x_updated"), 4 * r["nx"])

            def log1p(o, e, s, q, t):
                link(ts(t, e, 2.0, None, ALU.add))
                link(dve.reciprocal(s, t))
                link(tt(s, s, e, ALU.mult))
                link(tt(q, s, s, ALU.mult))
                link(ts(o, q, 2.0 / 17, 2.0 / 15, ALU.mult, ALU.add))
                for d in (13, 11, 9, 7, 5, 3, 1):
                    link(tt(o, o, q, ALU.mult))
                    link(ts(o, o, 2.0 / d, None, ALU.add))
                link(tt(o, o, s, ALU.mult))

            def gate_rows(r):
                l = r["l"]
                g = gt
                dve.memset(gd_in[:, :, 0:3], 0.0)
                dve.memset(rg_in[:, :, 0:3], 0.0)
                ts(g[2], g[0], c("dt_rows", l, 1, 8), None, ALU.add).then_inc(sem("gates_z"), 1)
                dve.wait_ge(sem("gates_e"), l + 1)
                log1p(g[5], g[4], g[6], g[7], g[8])
                link(stt(g[5], g[2], 0.0, g[5], ALU.max, ALU.add))
                link(ts(g[5], g[5], neg_a[:, l:l + 1], None, ALU.mult))
                for j in range(NT):
                    s = slice(P * j, P * j + P)
                    ins = dve.tensor_tensor_scan(g[6][:, s], k("ones", 0, P, 8), g[5][:, s], 0.0, ALU.mult, ALU.add)
                link(ins)
                link(ts(g[7], g[6], k("sel_g", 0, 1, 8), None, ALU.mult))
                stt(gates_c[:, :], g[1], k("sel_beta", 0, 1, 8), g[7], ALU.mult, ALU.add).then_inc(sem("gates_ready"), 1)

            def spread(r):
                l = r["l"]
                dve.wait_ge(sem("gates_spread"), l + 1)
                link(dve.tensor_copy(gcol, aux[:, 0:16]))
                dve.tensor_copy(rbeta, acc[:, 0:1024].rearrange("p (h t) -> p h t", t=T))
                for j in range(NT):
                    for h in range(GD_H):
                        ins = stt(dt_[:, j, P * h:P * h + P], acc[:, 1024 + T * h + P * j:1024 + T * h + P * j + P],
                                  gcol[:, 8 * j + 4 + h:8 * j + 5 + h], k("neg", 0, P), ALU.subtract, ALU.add)
                ins.then_inc(sem("gates_diff"), 1)

            def conv(dst, src, w, b=None):
                if b is None:
                    link(ts(dst, src[:, 0:T], w(0), None, ALU.mult))
                else:
                    link(ts(dst, src[:, 0:T], w(0), b, ALU.mult, ALU.add))
                for i in range(1, 4):
                    ins = stt(dst, src[:, i:i + T], w(i), dst, ALU.mult, ALU.add)
                    if i < 3:
                        link(ins)
                return ins

            def rg_conv(r):
                l = r["l"]
                dve.wait_ge(sem("act_evac"), r["evac"])
                for t in range(2):
                    ins = conv(xc[:, t, :], rg_in[:, t, :], lambda i: c("rg_conv_w", 8 * l + 2 * i + t), c("rg_conv_b", 2 * l + t))
                ins.then_inc(sem("rg_xc"), 1)

            def gd_conv(r):
                l = r["l"]
                dve.wait_ge(sem("act_evac"), r["evac"])
                for i in (2 * r["i"], 2 * r["i"] + 1):
                    ins = conv(qkv[:, i, :], gd_in[:, i, :], lambda t: c("gd_conv_w", 48 * l + 12 * t + i))
                ins.then_inc(sem("gd_conv"), 1)

            def gd_ss(r):
                l = r["l"]
                dve.wait_ge(sem("gd_rn"), l + 1)
                tt(qkv[:, 0:8, :], qkv[:, 0:8, :], sq[:, :, :], ALU.mult).then_inc(sem("gd_qk"), 1)

            def rg_scan(r):
                l = r["l"]
                dve.wait_ge(sem("rg_tanh"), l + 1)
                ts(rsq, rt, 1e-19, None, ALU.max).then_inc(sem("rg_tc"), 1)
                dve.wait_ge(sem("rg_tc"), l + 1)
                link(ts(rrcp, rt, 1.0, None, ALU.add))
                link(dve.reciprocal(rrcp, rrcp))
                ra, rbx, rh = rt, r_ig[:, 2:4, :], r_ig[:, 0:2, :]
                link(ts(ra, rt, -1.0, 1.0, ALU.mult, ALU.add))
                link(tt(ra, ra, rrcp, ALU.mult))
                link(tt(rbx, rbx, xc, ALU.mult))
                link(tt(rbx, rbx, rrcp, ALU.mult))
                dve.wait_ge(sem("rg_root"), l + 1)
                link(stt(rbx, rsq, 2.0, rbx, ALU.mult, ALU.mult))
                for t in range(2):
                    ins = dve.tensor_tensor_scan(rh[:, t, :], ra[:, t, :], rbx[:, t, :], 0.0, ALU.mult, ALU.add)
                link(ins)
                dve.wait_ge(sem("act_evac"), r["evac"])
                link(tt(u32[:, 6:8, :], rh, rgate, ALU.mult))

            def gd_scores(r):
                l = r["l"]
                dve.wait_ge(sem("gates_read"), l + 1)
                dve.wait_ge(sem("gd_qk"), l + 1)
                link(tt(eq, qkv[:, 0:4, P:T], eq, ALU.mult))
                dve.tensor_copy(dlast, dt_[:, 0, :].rearrange("p (h t) -> p h t", t=P)[:, :, P - 1])
                dve.wait_ge(sem("gd_scores"), l + 1)
                for j in range(NT):
                    link(tt(lt[:, j, :], bank[j], dt_[:, j, :], ALU.mult))
                    rb = rbeta[:, :, P * j:P * j + P]
                    l4 = lt[:, j, :].rearrange("p (h t) -> p h t", t=P)
                    tt(sc[:, j, :], bank[2 + j], dt_[:, j, :], ALU.mult)
                    link(tt(l4, l4, rb, ALU.mult))
                    x4 = xt[:, j, :].rearrange("p (h t) -> p h t", t=P)
                    n4 = ntm[:, j, :].rearrange("p (h t) -> p h t", t=P)
                    link(tt(n4, l4, bc(k("masks", 6 * P, P), 1, 4), ALU.mult))
                    tt(x4, bc(ident, 1, 4), n4, ALU.subtract).then_inc(sem("gd_x"), 1)

            def gd_y(r):
                l, i = r["l"], r["i"]
                for j in range(NT):
                    l4 = lt[:, j, :].rearrange("p (h t) -> p h t", t=P)
                    n4 = ntm[:, j, :].rearrange("p (h t) -> p h t", t=P)
                    m = bc(k("masks", (6 - i) * P, P), 1, 4)
                    if i == 1:
                        dve.wait_ge(sem("gd_x0"), 2 * l + j + 1)
                        tt(n4, l4, m, ALU.mult)
                        dve.tensor_copy(xi[:, j, :], bank[j]).then_inc(sem("gd_x"), 1)
                    else:
                        dve.wait_ge(sem("gd_z"), 12 * l + 2 * (i - 2) + j + 1)
                        tt(n4, l4, m, ALU.mult)
                        tt(xi[:, j, :], xi[:, j, :], bank[j], ALU.subtract)
                        ins = tt(xt[:, j, :], xt[:, j, :], bank[2 + j], ALU.subtract)
                        ins.then_inc(sem("gd_x"), 1)

            def hg_prep(r):
                l = r["l"]
                dve.wait_ge(sem("act_evac"), r["evac"])
                for t in range(2):
                    ins = ts(hf[:, t, :], hf[:, t, :], omlb[:, 2 * l + t:2 * l + t + 1], lbv[:, 2 * l + t:2 * l + t + 1], ALU.mult, ALU.add)
                link(ins)
                ts(hcum, hf, 1e-19, None, ALU.max).then_inc(sem("hg_f"), 1)
                ts(hk, hf, -1.0, 1.0, ALU.mult, ALU.add)
                dve.memset(hat, 0.0)
                link(ts(hq, hq, HG_D ** -0.5, None, ALU.mult))
                dve.wait_ge(sem("hg_logf"), l + 1)
                for t in range(2):
                    ins = dve.tensor_tensor_scan(hf[:, t, :], k("ones").broadcast_to([P, T]), hcum[:, t, :], 0.0, ALU.mult, ALU.add)
                link(ins)

            def by_block(v, n):
                return v.rearrange("p a b -> p (a b)").rearrange("p (b two n) -> p b two n", two=2, n=n)

            def hg_exponents(r):
                l, i = r["l"], r["n"]
                n = ([P] + LEVELS)[i]
                if i >= 4:
                    dve.wait_ge(sem("hg_scores"), 9 * l + i - 3)
                cv = by_block(hf, n)
                dv = de[:, i % 4, :].rearrange("p (b two n) -> p b two n", two=2, n=n)
                mid = bc(cv[:, :, 0, n - 1], 2, n)
                tt(dv[:, :, 1, :], cv[:, :, 1, :], mid, ALU.subtract)
                tt(dv[:, :, 0, :], mid, cv[:, :, 0, :], ALU.subtract).then_inc(sem("hg_de"), 1)

            def hg_products(l, i):
                n = ([P] + LEVELS)[i]
                dve.wait_ge(sem("hg_e"), 8 * l + i + 1)
                dv = de[:, i % 4, :].rearrange("p (b two n) -> p b two n", two=2, n=n)
                tt(dv[:, :, 1, :], dv[:, :, 1, :], by_block(hq, n)[:, :, 1, :], ALU.mult)
                tt(dv[:, :, 0, :], dv[:, :, 0, :], by_block(hk, n)[:, :, 0, :], ALU.mult).then_inc(sem("hg_qk"), 1)

            def hg_collect(l, n):
                dve.wait_ge(sem("hg_scores"), 9 * l + n + 1)
                for par in range(2):
                    b = hg_scores[2 * (n % 2) + par]
                    if n == 0:
                        ins = dve.tensor_copy(hax[:, par, :], b[:, 0:2 * P])
                    else:
                        m = ident if n == 8 else k("masks", P * (n - 1), P)
                        ins = dve.copy_predicated(hat[:, par, :, :], bc(m.bitcast(I32), 1, 4),
                                                  b.rearrange("p (a b) -> p a b", b=P))
                ins.then_inc(sem("hg_copied"), 1)
                dve.wait_ge(sem("hg_copied"), 9 * l + n + 1)

            def hg_level(r):
                l, n = r["l"], r["n"]
                if n == 0:
                    hg_products(l, 0)
                if n + 1 < 8:
                    hg_products(l, n + 1)
                if n:
                    hg_collect(l, n - 1)

            def hg_out(r):
                l = r["l"]
                hg_collect(l, 8)
                for j in range(NT):
                    dve.wait_ge(sem("gd_z"), 12 * l + 10 + j + 1)
                    ins = tt(xt[:, j, :], xt[:, j, :], bank[2 + j], ALU.subtract)
                ins.then_inc(sem("gd_vfree"), 1)
                dve.wait_ge(sem("gd_vfree"), l + 1)

            def gd_chunks(r):
                l = r["l"]
                dve.wait_ge(sem("gd_tok"), 3 * l + 3)
                v4 = [vtok[:, j, :].rearrange("p (h t) -> p h t", t=P) for j in range(2)]

                def col(v):
                    return bc(v, 2, P)

                def beta(j):
                    return col(gcol[:, 8 * j:8 * j + 4])

                tt(rr, v4[0], beta(0), ALU.mult).then_inc(sem("gd_r"), 1)
                dve.wait_ge(sem("gd_vn"), 2 * l + 1)
                tt(vs, bank[0].rearrange("p (h t) -> p h t", t=P), col(dlast), ALU.mult).then_inc(sem("gd_vs"), 1)
                dve.tensor_copy(vn[:, 0, :], bank[0])
                dve.wait_ge(sem("hg_rstd"), l + 1)
                for t in range(2):
                    ins = stt(u32[:, t, :], ho[:, t, :], c("hg_norm_w", l), hrs[:, T * t:T * t + T], ALU.mult, ALU.mult)
                link(ins)
                link(tt(u32[:, 0:2, :], u32[:, 0:2, :], hgate, ALU.mult))
                dve.wait_ge(sem("gd_ks"), l + 1)
                link(tt(tmp, bank[2].rearrange("p (h t) -> p h t", t=P), col(gexp), ALU.mult))
                link(tt(tmp, v4[1], tmp, ALU.subtract))
                tt(rr, tmp, beta(1), ALU.mult).then_inc(sem("gd_r"), 1)
                dve.wait_ge(sem("gd_vn"), 2 * l + 2)
                dve.tensor_copy(vn[:, 1, :], bank[3]).then_inc(sem("gd_vn_copied"), 1)
                dve.wait_ge(sem("gd_orstd"), l + 1)
                link(stt(u32[:, 2:6, :], go, c("gd_norm_w", l), grs, ALU.mult, ALU.mult))
                tt(u32[:, 2:6, :], u32[:, 2:6, :], z, ALU.mult).then_inc(sem("u32_ready"), 1)

            def reduced(o, tmp_, shift_turns, shift):
                magic = 12582912.0
                link(ts(o, tmp_, 1.0 / (2 * np.pi), shift_turns, ALU.mult, ALU.add))
                link(ts(o, o, magic, None, ALU.add))
                return ts(o, o, magic, None, ALU.subtract)

            def angles(ang, turns, o, shift_turns, shift):
                link(reduced(turns, ang, shift_turns, shift))
                c1, c2 = 6.28125, float(np.float32(2 * np.pi - 6.28125))
                c3 = float(2 * np.pi - 6.28125 - np.float64(np.float32(2 * np.pi - 6.28125)))
                link(stt(o, turns, -c1, ang, ALU.mult, ALU.add))
                link(stt(o, turns, -c2, o, ALU.mult, ALU.add))
                link(stt(o, turns, -c3, o, ALU.mult, ALU.add))
                link(ts(o, o, shift, 3.1415925, ALU.add, ALU.min))
                return ts(o, o, -3.1415925, None, ALU.max)

            def ret_tables(r):
                dve.wait_ge(sem("pos_loaded"), 16)
                dve.wait_ge(sem("posc_loaded"), 16)
                link(dve.tensor_copy(angt[:, 2, :], posf.bitcast(I32)))
                link(ts(angt[:, 2, :], angt[:, 2, :], k("inv_freq"), None, ALU.mult))
                link(angles(angt[:, 2, :], angt[:, 3, :], angt[:, 0, :], 0.0, 0.0))
                angles(angt[:, 2, :], angt[:, 3, :], angt[:, 1, :], 0.25, float(np.pi / 2)).then_inc(sem("ret_angles"), 1)

            def rope(r):
                dve.wait_ge(sem("ret_sincos"), 1)
                dve.wait_ge(sem("act_evac"), r["evac"])
                s4, c4 = bc(csin, 1, 4), bc(ccos, 1, 4)
                a, b = sq[:, 0:4, :], sq[:, 4:8, :]
                for i in range(2):
                    v = rqk[:, 8 * i:8 * i + 8, :].rearrange("p (h two) t -> p h two t", two=2)
                    x1, x2 = v[:, :, 0, :], v[:, :, 1, :]
                    tt(a, x1, s4, ALU.mult)
                    link(tt(b, x2, s4, ALU.mult))
                    tt(x1, x1, c4, ALU.mult)
                    link(tt(x2, x2, c4, ALU.mult))
                    tt(x1, x1, b, ALU.subtract)
                    tt(x2, x2, a, ALU.add).then_inc(sem("roped"), 1)
                    dve.wait_ge(sem("roped"), i + 1)

            def ret_scores(r):
                h = r["h"]
                if h == 0:
                    dve.wait_ge(sem("dec_loaded"), 16)
                dve.wait_ge(sem("ret_scores"), h + 1)
                tt(rp[:, h % 2, :], aux[:, 0:3 * P], dec[:, h, :], ALU.mult).then_inc(sem("ret_p_ready"), 1)

            def ret_norm(r):
                h = r["h"]
                dve.wait_ge(sem("ret_r_ready"), h + 1)
                y = ry[h % 2]
                link(tt(y, y, bc(rstd[:, :], 1, 4), ALU.mult))
                tt(y, y, rg[:, 4 * h:4 * h + 4, :], ALU.mult).then_inc(sem("ret_y_ready"), 1)
                dve.wait_ge(sem("ret_y_ready"), h + 1)

            def ya_(r):
                dve.wait_ge(sem("panel_used"), r["panel"])
                dve.tensor_copy(ya.rearrange("p a b -> p (a b)"), acc[:, :]).then_inc(sem("ya_ready"), 1)
                dve.wait_ge(sem("ya_ready"), 1)

            def dil_tables(r):
                n = NT * DIL_HALF
                link(dve.tensor_copy(small[:, 42:44], posc.bitcast(I32)))
                for j in range(NT):
                    ins = ts(dang[:, 2, DIL_HALF * j:DIL_HALF * (j + 1)], k("freqs", 0, DIL_HALF), small[:, 42 + j:43 + j], None, ALU.mult)
                link(ins)
                link(angles(dang[:, 2, :], dang[:, 3, :], dang[:, 0, :], 0.0, 0.0))
                angles(dang[:, 2, :], dang[:, 3, :], dang[:, 1, :], 0.25, float(np.pi / 2)).then_inc(sem("dil_angles"), 1)

            def dil_rope(r):
                i = r["i"]
                dve.wait_ge(sem("dil_sincos"), 1)
                dve.wait_ge(sem("act_evac"), r["evac"])
                for j in range(NT):
                    v = dtok[:, i % 2, PC * j:PC * j + PC].rearrange("p (h d) -> p h d", d=DIL_D)
                    x1, x2 = v[:, :, 0:DIL_HALF], v[:, :, DIL_HALF:2 * DIL_HALF]
                    s = bc(dcs[:, 0, DIL_HALF * j:DIL_HALF * (j + 1)], 1, 4)
                    co = bc(dcs[:, 1, DIL_HALF * j:DIL_HALF * (j + 1)], 1, 4)
                    a = drop[:, 2 * j, 0:32].rearrange("p (h d) -> p h d", d=DIL_HALF)
                    b = drop[:, 2 * j + 1, 0:32].rearrange("p (h d) -> p h d", d=DIL_HALF)
                    tt(a, x1, s, ALU.mult)
                    link(tt(b, x2, s, ALU.mult))
                    tt(x1, x1, co, ALU.mult)
                    link(tt(x2, x2, co, ALU.mult))
                    tt(x1, x1, b, ALU.subtract)
                    ins = tt(x2, x2, a, ALU.add)
                ins.then_inc(sem("dil_roped"), 1)

            def dil(r):
                dve.wait_ge(sem("dmask_loaded"), 16)
                for a in range(DIL_S):
                    dve.wait_ge(sem("dil_scores"), a + 1)
                    if a >= 2:
                        dve.wait_ge(sem("dil_p_turned"), a - 1)
                    d = ds_[a % 2]
                    stt(d[:, 0:3 * P], acc[:, 0:3 * P], DIL_D ** -0.5, dmask[:, 0:3 * P], ALU.mult, ALU.add)
                    stt(d[:, 3 * P:9 * P], acc[:, 512:512 + 6 * P], DIL_D ** -0.5, dmask[:, 3 * P:9 * P], ALU.mult, ALU.add)\
                        .then_inc(sem("dil_masked"), 1)
                    dve.wait_ge(sem("dil_masked"), a + 1)
                    dve.tensor_reduce(dmax[:, 2 * a:2 * a + 1], d[:, 0:3 * P], AX.X, ALU.max)
                    link(dve.tensor_reduce(dmax[:, 2 * a + 1:2 * a + 2], d[:, 3 * P:9 * P], AX.X, ALU.max))
                    ts(dneg[:, 2 * a:2 * a + 2], dmax[:, 2 * a:2 * a + 2], -1.0, None, ALU.mult).then_inc(sem("dil_max"), 1)
                dve.wait_ge(sem("dil_p"), DIL_S)
                link(dve.reciprocal(drinv, drow))
                dve.wait_ge(sem("dil_pv"), DIL_S)
                for j in range(NT):
                    o = (bank[3] if j == 0 else aux[:, :]).rearrange("p (a d) -> p a d", d=DIL_D)
                    ins = tt(do[:, j, :].rearrange("p (a d) -> p a d", d=DIL_D), o,
                             bc(drinv[:, 8 * j:8 * j + 8], 2, DIL_D), ALU.mult)
                ins.then_inc(sem("dil_o"), 1)
                dve.wait_ge(sem("dil_o_turned"), 1)
                for i in range(2):
                    dve.tensor_copy(u32[:, 2 * i:2 * i + 2, :].rearrange("p a b -> p (a b)"), bank[i]).then_inc(sem("dil_ot"), 1)
                dve.wait_ge(sem("dil_ot"), 2)

            def gate_ya(r):
                i = r["i"]
                dve.wait_ge(sem("act_evac"), r["evac"])
                s = ya[:, 2 * i:2 * i + 2, :].rearrange("p a b -> p (a b)")
                tt(s, s, act_t[:, i % 2, :], ALU.mult).then_inc(sem("ya_gated"), 1)

            def mixed(r):
                dve.wait_ge(sem("act_evac"), r["evac"])
                dve.wait_ge(sem("ya_gated"), 4)
                dve.wait_ge(sem("panel_used"), r["panel"])
                flat = sga.rearrange("p a b -> p (a b)")
                tt(flat, flat, acc[:, :], ALU.mult).then_inc(sem("acc_mixed"), 1)
                dve.wait_ge(sem("acc_mixed"), 1)
                tt(u32[:, :, :], sga, ya, ALU.add).then_inc(sem("u32_ready"), 1)

            def ple(r):
                dve.wait_ge(sem("act_evac"), r["evac"])
                dve.wait_ge(sem("panel_used"), r["panel"])
                for b in range(4):
                    g = gate_t[:, 2 * b:2 * b + 2, :].rearrange("p a b -> p (a b)")
                    tt(g, g, bank[b], ALU.mult).then_inc(sem("gated_ready"), 1)

            run = {"panel": panel, "op_lo": op_lo_, "fill": fill, "x_update": x_update, "gate_rows": gate_rows,
                   "rg_conv": rg_conv, "gd_conv": gd_conv, "gd_ss": gd_ss, "rg_scan": rg_scan, "spread": spread,
                   "gd_scores": gd_scores, "gd_y": gd_y, "hg_prep": hg_prep, "hg_exponents": hg_exponents,
                   "hg_level": hg_level, "hg_out": hg_out, "gd_chunks": gd_chunks, "ret_tables": ret_tables,
                   "rope": rope, "ret_scores": ret_scores, "ret_norm": ret_norm, "ya": ya_,
                   "dil_tables": dil_tables, "dil_rope": dil_rope, "dil": dil, "gate_ya": gate_ya, "mixed": mixed,
                   "ple": ple, "relu2": relu2}

            dve.memset(bias_eps, EPS)
            dve.memset(bias_lndk, float(np.log(GD_D ** -0.5)))
            dve.wait_ge(sem("cols_loaded"), 16)
            dve.wait_ge(sem("cst_loaded"), 16)
            lam = c("rg_lambda", 0, 4)
            link(ts(small[:, 32 + 4:40], lam, -1.0, None, ALU.mult))
            link(tt(small[:, 36:40], small[:, 36:40], lam, ALU.max))
            lb = c("hg_lb", 0, 4)
            link(tt(small[:, 116:118], lb[:, 0:2], lb[:, 2:4], ALU.max))
            tt(small[:, 112:114], lb[:, 0:2], small[:, 116:118], ALU.subtract)
            tt(small[:, 114:116], lb[:, 2:4], small[:, 116:118], ALU.subtract).then_inc(sem("setup_a"), 1)
            dve.wait_ge(sem("setup_e"), 1)
            ts(neg_a, small[0:8, 34:36], -1.0, None, ALU.mult)
            log1p(small[:, 120:124], small[:, 36:40], small[:, 124:128], small[:, 128:132], small[:, 132:136])
            link(ts(small[:, 124:128], lam, -1.0, 0.0, ALU.mult, ALU.max))
            link(tt(sp4, small[:, 120:124], small[:, 124:128], ALU.add))
            link(ts(sp4, sp4, 4.0, None, ALU.mult))
            e0, e1 = small[:, 112:114], small[:, 114:116]
            link(tt(small[:, 116:118], e0, e1, ALU.add))
            link(dve.reciprocal(small[:, 118:120], small[:, 116:118]))
            tt(e0, e0, small[:, 118:120], ALU.mult)
            link(tt(e1, e1, small[:, 118:120], ALU.mult))
            dve.memset(lbv[:, 0:2], 0.0)
            link(tt(e1, e0, e1, ALU.add))
            link(tt(lbv[:, 2:4], e1, e0, ALU.subtract))
            link(ts(omlb, lbv, -1.0, 1.0, ALU.mult, ALU.add))
            for what, r in schedule:
                if what in run:
                    run[what](r)


def kernel(**inputs):
    import concourse.bacc as bacc
    from concourse.bass_utils import run_bass_kernel_spmd as run

    i = {n: np.asarray(a) for n, a in inputs.items()}
    f = np.float32

    def columns(a, n):
        return np.ascontiguousarray(a.reshape(-1, P).T)

    def rows(a):
        o = np.zeros((P, DEPTH), f)
        o[GD_H:2 * GD_H] = a.T
        return o

    tab = {n: columns(i[n], 0) for n, _ in COLS if n in i and n not in ("hg_norm_w",)}
    tab["hg_norm_w"] = np.ascontiguousarray(np.concatenate([i["hg_norm_w"]] * 2, 1).T)
    tab["dt_rows"], tab["a_log_rows"] = rows(i["gd_dt_bias"]), rows(i["gd_a_log"])
    rg_w = np.zeros((P, DEPTH, 2, 2, P), f)
    for g, name in enumerate(("rg_wr", "rg_wi")):
        for n in range(4):
            s = slice(64 * (n % 2), 64 * (n % 2) + 64)
            for l in range(DEPTH):
                rg_w[s, l, g, n // 2, s] = i[name][l, n]
    cst, decay, dil_mask = shape_constants()
    data = {
        "x_t": i["x"][0].T.reshape(KD, P, T).transpose(1, 0, 2),
        "p_t": i["p_2"][0, 0].T.reshape(2, P, T).transpose(1, 0, 2),
        "columns": np.concatenate([tab[n] for n, _ in COLS], 1), "constants": cst, "decay": decay,
        "dil_mask": dil_mask, "rg_w": rg_w.reshape(P, -1), "positions": i["positions_2"],
        "positions_c": i["positions_2"].reshape(NT, P).T,
    }
    for n in ("ffn1_gate", "ffn1_up", "ffn1_down", "w_in", "w_out", "ffn2_gate", "ffn2_up", "ffn2_down", "w_in_2",
              "w_ret_out_2", "w_dil_out_2", "w_o_2", "w_up_2", "w_down_2", "w_ple_gate_2", "w_ple_in_2"):
        data[n] = i[n]
    nc = bacc.Bacc("TRN2", target_bir_lowering=False, num_devices=1)
    data = {n: np.ascontiguousarray(a) for n, a in data.items()}
    ap = {n: nc.dram_tensor(n, a.shape, mybir.dt.from_np(a.dtype), kind="ExternalInput").ap() for n, a in data.items()}
    out = nc.dram_tensor("out", (P, KD, T), F32, kind="ExternalOutput").ap()
    build(nc, ap, out)
    r = run(nc, [data], core_ids=[0])
    y = r.results[0]["out"]
    return np.ascontiguousarray(y.transpose(2, 1, 0).reshape(1, T, D))
```
